# Optimizing a Trainium2 kernel written in Bass

```python
import math
import jax, jax.numpy as jnp
from jax import lax
import numpy as np

D_MODEL = 1024
BATCH = 1
SEQ = 512
DEPTH = 1

CHUNK = 64
N_MIXERS = 3
N_LAYERS_A = len(range(0, DEPTH, N_MIXERS))
N_LAYERS_B = len(range(1, DEPTH, N_MIXERS))
N_LAYERS_C = len(range(2, DEPTH, N_MIXERS))
RMS_EPS = 1e-6
D_FF = 4 * D_MODEL
CONV_W = 4

GDN_DK = 128
GDN_DV = 128
GDN_HEADS = D_MODEL // GDN_DK
GDN_QK = GDN_HEADS * GDN_DK
GDN_V = GDN_HEADS * GDN_DV
GDN_CONV_CH = 2 * GDN_QK + GDN_V
GDN_IN = GDN_CONV_CH + GDN_V + 2 * GDN_HEADS

S5_GROUP = 16
S5_GROUPS = D_MODEL // S5_GROUP
S5_STATE = 64

M2_INNER = 2 * D_MODEL
M2_HEAD_DIM = 64
M2_HEADS = M2_INNER // M2_HEAD_DIM
M2_GROUPS = 8
M2_HPG = M2_HEADS // M2_GROUPS
M2_STATE = 128
M2_BC = M2_GROUPS * M2_STATE
M2_CONV_CH = M2_INNER + 2 * M2_BC
M2_IN = M2_INNER + M2_CONV_CH + M2_HEADS


def rmsnorm(x, g):
    xf = x.astype(jnp.float32)
    y = xf * lax.rsqrt(jnp.mean(xf * xf, axis=-1, keepdims=True) + RMS_EPS)
    return (y * g.astype(jnp.float32)).astype(x.dtype)

def causal_dwconv(x, w):
    return lax.conv_general_dilated(
        x, w[:, None, :], window_strides=(1,), padding=[(w.shape[0] - 1, 0)],
        dimension_numbers=("NWC", "WIO", "NWC"), feature_group_count=x.shape[-1])

def l2norm(t):
    return t * lax.rsqrt(jnp.sum(t * t, axis=-1, keepdims=True) + 1e-6)

def gated_deltanet(h, w_in, conv_w, a_log, dt_bias, o_norm_g, w_out):
    bsz, L, _ = h.shape
    nc = L // CHUNK
    f32 = jnp.float32
    proj = h @ w_in
    qkv, gate, a_raw, b_raw = jnp.split(
        proj, [GDN_CONV_CH, GDN_CONV_CH + GDN_V, GDN_CONV_CH + GDN_V + GDN_HEADS], axis=-1)
    qkv = jax.nn.silu(causal_dwconv(qkv, conv_w)).astype(f32)
    q, k, v = jnp.split(qkv, [GDN_QK, 2 * GDN_QK], axis=-1)
    q = l2norm(q.reshape(bsz, L, GDN_HEADS, GDN_DK)) * (GDN_DK ** -0.5)
    k = l2norm(k.reshape(bsz, L, GDN_HEADS, GDN_DK))
    v = v.reshape(bsz, L, GDN_HEADS, GDN_DV)
    g = -jnp.exp(a_log.astype(f32)) * jax.nn.softplus(a_raw.astype(f32) + dt_bias.astype(f32))
    beta = jax.nn.sigmoid(b_raw.astype(f32))

    def to_chunks(t):
        return t.reshape(bsz, nc, CHUNK, GDN_HEADS, -1).transpose(0, 3, 1, 2, 4)

    qc, kc, vc = to_chunks(q), to_chunks(k), to_chunks(v)
    gc = g.reshape(bsz, nc, CHUNK, GDN_HEADS).transpose(0, 3, 1, 2)
    bc = beta.reshape(bsz, nc, CHUNK, GDN_HEADS).transpose(0, 3, 1, 2)
    G = jnp.cumsum(gc, axis=-1)
    idx = jnp.arange(CHUNK)
    causal = idx[:, None] >= idx[None, :]
    strict = idx[:, None] > idx[None, :]
    decay = jnp.exp(jnp.where(causal, G[..., :, None] - G[..., None, :], -jnp.inf))
    kk = jnp.einsum('bhcid,bhcjd->bhcij', kc, kc)
    tri = jnp.where(strict, bc[..., :, None] * kk * decay, 0.0) + jnp.eye(CHUNK, dtype=f32)
    rhs = jnp.concatenate([vc * bc[..., None], kc * (bc * jnp.exp(G))[..., None]], axis=-1)
    sol = lax.linalg.triangular_solve(tri, rhs, left_side=True, lower=True, unit_diagonal=True)
    u, w = sol[..., :GDN_DV], sol[..., GDN_DV:]
    qk = jnp.einsum('bhcid,bhcjd->bhcij', qc, kc) * decay
    q_dec = qc * jnp.exp(G)[..., None]
    k_dec = kc * jnp.exp(G[..., -1:] - G)[..., None]
    chunk_decay = jnp.exp(G[..., -1])
    xs = tuple(jnp.moveaxis(t, 2, 0) for t in (u, w, qk, q_dec, k_dec, chunk_decay))

    def step(S, inp):
        u_c, w_c, qk_c, qd_c, kd_c, cd_c = inp
        v_new = u_c - jnp.einsum('bhid,bhde->bhie', w_c, S)
        o = jnp.einsum('bhid,bhde->bhie', qd_c, S) + jnp.einsum('bhij,bhje->bhie', qk_c, v_new)
        S = cd_c[..., None, None] * S + jnp.einsum('bhid,bhie->bhde', kd_c, v_new)
        return S, o

    S0 = jnp.zeros((bsz, GDN_HEADS, GDN_DK, GDN_DV), f32)
    _, o = lax.scan(step, S0, xs)
    o = o.transpose(1, 0, 3, 2, 4).reshape(bsz, L, GDN_HEADS, GDN_DV)
    o = rmsnorm(o, o_norm_g) * jax.nn.silu(gate.astype(f32).reshape(bsz, L, GDN_HEADS, GDN_DV))
    return o.reshape(bsz, L, GDN_V).astype(h.dtype) @ w_out

def s5_mixer(h, w_in, lam_re, lam_im, log_dt, b_re, b_im, c_re, c_im, d_skip, w_out):
    bsz, L, _ = h.shape
    f32 = jnp.float32
    u = (h @ w_in).astype(f32)
    ug = u.reshape(bsz, L, S5_GROUPS, S5_GROUP).transpose(1, 0, 2, 3)
    lam = lax.complex(lam_re.astype(f32), lam_im.astype(f32))
    dt = jnp.exp(log_dt.astype(f32))[:, None]
    lam_bar = jnp.exp(lam * dt)
    b_bar = ((lam_bar - 1.0) / lam)[..., None] * lax.complex(b_re.astype(f32), b_im.astype(f32))
    bu = jnp.einsum('gpk,lbgk->lbgp', b_bar, ug.astype(jnp.complex64))
    a = jnp.broadcast_to(lam_bar[None, None], (L, 1, S5_GROUPS, S5_STATE))

    def combine(e1, e2):
        a1, b1 = e1
        a2, b2 = e2
        return a1 * a2, a2 * b1 + b2

    _, states = lax.associative_scan(combine, (a, bu), axis=0)
    c = lax.complex(c_re.astype(f32), c_im.astype(f32))
    y = jnp.real(jnp.einsum('gkp,lbgp->lbgk', c, states)) \
        + d_skip.astype(f32).reshape(S5_GROUPS, S5_GROUP) * ug
    y = jax.nn.gelu(y.transpose(1, 0, 2, 3).reshape(bsz, L, D_MODEL)).astype(h.dtype)
    ag = y @ w_out
    val, gt = jnp.split(ag, 2, axis=-1)
    return val * jax.nn.sigmoid(gt)

def mamba2_mixer(h, w_in, conv_w, conv_b, dt_bias, a_log, d_skip, norm_g, w_out):
    bsz, L, _ = h.shape
    nc = L // CHUNK
    f32 = jnp.float32
    proj = h @ w_in
    z, xbc, dt_raw = jnp.split(proj, [M2_INNER, M2_INNER + M2_CONV_CH], axis=-1)
    xbc = jax.nn.silu(causal_dwconv(xbc, conv_w) + conv_b).astype(f32)
    xs, Bm, Cm = jnp.split(xbc, [M2_INNER, M2_INNER + M2_BC], axis=-1)
    x = xs.reshape(bsz, L, M2_HEADS, M2_HEAD_DIM)
    dt = jax.nn.softplus(dt_raw.astype(f32) + dt_bias.astype(f32))
    dA = dt * (-jnp.exp(a_log.astype(f32)))
    xdt = (x * dt[..., None]).reshape(bsz, nc, CHUNK, M2_GROUPS, M2_HPG, M2_HEAD_DIM)
    Bc = Bm.reshape(bsz, nc, CHUNK, M2_GROUPS, M2_STATE)
    Cc = Cm.reshape(bsz, nc, CHUNK, M2_GROUPS, M2_STATE)
    cum = jnp.cumsum(dA.reshape(bsz, nc, CHUNK, M2_GROUPS, M2_HPG), axis=2)
    idx = jnp.arange(CHUNK)
    causal = (idx[:, None] >= idx[None, :])[:, :, None, None]
    seg = cum[:, :, :, None] - cum[:, :, None, :]
    Lmat = jnp.exp(jnp.where(causal, seg, -jnp.inf))
    cb = jnp.einsum('bclgn,bcsgn->bclsg', Cc, Bc)
    y_diag = jnp.einsum('bclsgr,bcsgrp->bclgrp', cb[..., None] * Lmat, xdt)
    decay_states = jnp.exp(cum[:, :, -1:] - cum)
    states = jnp.einsum('bclgn,bclgrp->bcgrpn', Bc, xdt * decay_states[..., None])
    chunk_decay = jnp.exp(cum[:, :, -1])

    def step(S, inp):
        cd, st = inp
        return cd[..., None, None] * S + st, S

    S0 = jnp.zeros((bsz, M2_GROUPS, M2_HPG, M2_HEAD_DIM, M2_STATE), f32)
    _, S_prev = lax.scan(step, S0, (jnp.moveaxis(chunk_decay, 1, 0), jnp.moveaxis(states, 1, 0)))
    S_prev = jnp.moveaxis(S_prev, 0, 1)
    y_off = jnp.einsum('bclgn,bcgrpn->bclgrp', Cc, S_prev) * jnp.exp(cum)[..., None]
    y = (y_diag + y_off).reshape(bsz, L, M2_HEADS, M2_HEAD_DIM) + d_skip.astype(f32)[:, None] * x
    y = y.reshape(bsz, L, M2_INNER) * jax.nn.silu(z.astype(f32))
    y = rmsnorm(y.reshape(bsz, L, M2_GROUPS, M2_INNER // M2_GROUPS),
                norm_g.reshape(M2_GROUPS, M2_INNER // M2_GROUPS))
    return y.reshape(bsz, L, M2_INNER).astype(h.dtype) @ w_out

def sq_relu_mlp(h, w1, w2):
    return jnp.square(jax.nn.relu(h @ w1)) @ w2

def _inv_softplus_dt(key, shape):
    dt = jnp.exp(jax.random.uniform(key, shape, minval=math.log(1e-3), maxval=math.log(1e-1)))
    return dt + jnp.log(-jnp.expm1(-dt))

def first_inputs(seed: int = 0) -> dict:
    key = jax.random.key(seed)
    ks = jax.random.split(key, 32)
    nrm = jax.random.normal
    f32 = jnp.float32
    nA, nB, nC = N_LAYERS_A, N_LAYERS_B, N_LAYERS_C
    return {
        "x": nrm(ks[0], (BATCH, SEQ, D_MODEL), f32),
        "norm_mix_g": 1.0 + 0.02 * nrm(ks[1], (DEPTH, D_MODEL), f32),
        "norm_mlp_g": 1.0 + 0.02 * nrm(ks[2], (DEPTH, D_MODEL), f32),
        "mlp_w1": nrm(ks[3], (DEPTH, D_MODEL, D_FF), f32) * D_MODEL ** -0.5,
        "mlp_w2": nrm(ks[4], (DEPTH, D_FF, D_MODEL), f32) * D_FF ** -0.5,
        "gdn_w_in": nrm(ks[5], (nA, D_MODEL, GDN_IN), f32) * D_MODEL ** -0.5,
        "gdn_conv_w": nrm(ks[6], (nA, CONV_W, GDN_CONV_CH), f32) * CONV_W ** -0.5,
        "gdn_a_log": jnp.log(jax.random.uniform(ks[7], (nA, GDN_HEADS), minval=1.0, maxval=16.0)),
        "gdn_dt_bias": _inv_softplus_dt(ks[8], (nA, GDN_HEADS)),
        "gdn_o_norm_g": 1.0 + 0.02 * nrm(ks[9], (nA, GDN_DV), f32),
        "gdn_w_out": nrm(ks[10], (nA, GDN_V, D_MODEL), f32) * GDN_V ** -0.5,
        "s5_w_in": nrm(ks[11], (nB, D_MODEL, D_MODEL), f32) * D_MODEL ** -0.5,
        "s5_lam_re": -0.5 + 0.01 * nrm(ks[12], (nB, S5_GROUPS, S5_STATE), f32),
        "s5_lam_im": math.pi * jnp.arange(S5_STATE, dtype=f32) + 0.01 * nrm(ks[13], (nB, S5_GROUPS, S5_STATE), f32),
        "s5_log_dt": jax.random.uniform(ks[14], (nB, S5_GROUPS), minval=math.log(1e-3), maxval=math.log(1e-1)),
        "s5_b_re": nrm(ks[15], (nB, S5_GROUPS, S5_STATE, S5_GROUP), f32) * (2 * S5_GROUP) ** -0.5,
        "s5_b_im": nrm(ks[16], (nB, S5_GROUPS, S5_STATE, S5_GROUP), f32) * (2 * S5_GROUP) ** -0.5,
        "s5_c_re": nrm(ks[17], (nB, S5_GROUPS, S5_GROUP, S5_STATE), f32) * (2 * S5_STATE) ** -0.5 * 4.0,
        "s5_c_im": nrm(ks[18], (nB, S5_GROUPS, S5_GROUP, S5_STATE), f32) * (2 * S5_STATE) ** -0.5 * 4.0,
        "s5_d": nrm(ks[19], (nB, D_MODEL), f32),
        "s5_w_out": nrm(ks[20], (nB, D_MODEL, 2 * D_MODEL), f32) * D_MODEL ** -0.5,
        "m2_w_in": nrm(ks[21], (nC, D_MODEL, M2_IN), f32) * D_MODEL ** -0.5,
        "m2_conv_w": nrm(ks[22], (nC, CONV_W, M2_CONV_CH), f32) * CONV_W ** -0.5,
        "m2_conv_b": 0.02 * nrm(ks[23], (nC, M2_CONV_CH), f32),
        "m2_dt_bias": _inv_softplus_dt(ks[24], (nC, M2_HEADS)),
        "m2_a_log": jnp.log(jax.random.uniform(ks[25], (nC, M2_HEADS), minval=1.0, maxval=16.0)),
        "m2_d": 1.0 + 0.02 * nrm(ks[26], (nC, M2_HEADS), f32),
        "m2_norm_g": 1.0 + 0.02 * nrm(ks[27], (nC, M2_INNER), f32),
        "m2_w_out": nrm(ks[28], (nC, M2_INNER, D_MODEL), f32) * M2_INNER ** -0.5,
        "final_norm_g": 1.0 + 0.02 * nrm(ks[29], (D_MODEL,), f32),
    }

def first_block(x, norm_mix_g, norm_mlp_g, mlp_w1, mlp_w2,
              gdn_w_in, gdn_conv_w, gdn_a_log, gdn_dt_bias, gdn_o_norm_g, gdn_w_out,
              s5_w_in, s5_lam_re, s5_lam_im, s5_log_dt, s5_b_re, s5_b_im, s5_c_re, s5_c_im, s5_d, s5_w_out,
              m2_w_in, m2_conv_w, m2_conv_b, m2_dt_bias, m2_a_log, m2_d, m2_norm_g, m2_w_out,
              final_norm_g):
    h = x
    for i in range(DEPTH):
        kind, j = i % N_MIXERS, i // N_MIXERS
        hn = rmsnorm(h, norm_mix_g[i])
        if kind == 0:
            m = gated_deltanet(hn, gdn_w_in[j], gdn_conv_w[j], gdn_a_log[j], gdn_dt_bias[j],
                               gdn_o_norm_g[j], gdn_w_out[j])
        elif kind == 1:
            m = s5_mixer(hn, s5_w_in[j], s5_lam_re[j], s5_lam_im[j], s5_log_dt[j], s5_b_re[j],
                         s5_b_im[j], s5_c_re[j], s5_c_im[j], s5_d[j], s5_w_out[j])
        else:
            m = mamba2_mixer(hn, m2_w_in[j], m2_conv_w[j], m2_conv_b[j], m2_dt_bias[j], m2_a_log[j],
                             m2_d[j], m2_norm_g[j], m2_w_out[j])
        h = h + m.astype(h.dtype)
        h = h + sq_relu_mlp(rmsnorm(h, norm_mlp_g[i]), mlp_w1[i], mlp_w2[i]).astype(h.dtype)
    return rmsnorm(h, final_norm_g)


HEAD_DIM = 64
CONV_HEADS = 4
ATTN_HEADS = 8
SGU_HEADS = 4
CONV_W_2 = CONV_HEADS * HEAD_DIM
ATTN_W = ATTN_HEADS * HEAD_DIM
SGU_W = SGU_HEADS * HEAD_DIM
D_MIX = CONV_W_2 + ATTN_W + SGU_W
D_IN_PROJ = 3 * CONV_W_2 + 3 * ATTN_W + 2 * SGU_W
CONV_WIDTH = 3
Q_BLOCK = 128
CHUNK_2 = 128
D_FF_2 = 4 * D_MODEL
PLE_DIM = 256
EPS = 1e-6


def rms_norm(x, g):
    xf = x.astype(jnp.float32)
    y = xf * lax.rsqrt(jnp.mean(xf * xf, axis=-1, keepdims=True) + EPS)
    return (y * g.astype(jnp.float32)).astype(x.dtype)

def short_conv(x, w):
    s = x.shape[1]
    xp = jnp.pad(x, ((0, 0), (CONV_WIDTH - 1, 0), (0, 0)))
    out = w[0] * xp[:, 0:s]
    for j in range(1, CONV_WIDTH):
        out = out + w[j] * xp[:, j:j + s]
    return out

def stick_breaking_attention(q, k, v):
    s_len = q.shape[1]
    scale = HEAD_DIM ** -0.5
    outs = []
    for qb in range(s_len // Q_BLOCK):
        start = qb * Q_BLOCK
        end = start + Q_BLOCK
        qi = q[:, start:end].astype(jnp.float32)
        kj = k[:, :end].astype(jnp.float32)
        vj = v[:, :end].astype(jnp.float32)
        z = jnp.einsum('bqhd,bkhd->bhqk', qi, kj) * scale
        t_pos = start + jnp.arange(Q_BLOCK)[:, None]
        s_pos = jnp.arange(end)[None, :]
        causal = s_pos < t_pos
        log_beta = jax.nn.log_sigmoid(z)
        log_rem = jnp.where(causal, jax.nn.log_sigmoid(-z), 0.0)
        suffix = lax.cumsum(log_rem, axis=3, reverse=True) - log_rem
        weights = jnp.where(causal, jnp.exp(log_beta + suffix), 0.0)
        o = jnp.einsum('bhqk,bkhd->bqhd', weights, vj)
        outs.append(o.astype(v.dtype))
    return jnp.concatenate(outs, axis=1)

def spatial_gating(u, v, g_v, w_s, b_s):
    bsz, s_len, _ = u.shape
    v = v.reshape(bsz, s_len, SGU_HEADS, HEAD_DIM)
    v = rms_norm(v, g_v.reshape(SGU_HEADS, HEAD_DIM))
    v = v.reshape(bsz, s_len // CHUNK_2, CHUNK_2, SGU_HEADS, HEAD_DIM)
    mask = jnp.tril(jnp.ones((CHUNK_2, CHUNK_2), dtype=w_s.dtype))
    w = w_s * mask
    sv = jnp.einsum('gts,bcsge->bctge', w, v) + b_s.T[:, :, None]
    return u * sv.reshape(bsz, s_len, SGU_W)

def second_inputs(seed: int = 0) -> dict:
    key = jax.random.key(seed)
    ks = jax.random.split(key, 17)

    def nrm(k, shape, scale):
        return jax.random.normal(k, shape, jnp.float32) * scale

    def gain(k, shape):
        return 1.0 + 0.05 * jax.random.normal(k, shape, jnp.float32)

    return {
        "x": nrm(ks[0], (BATCH, SEQ, D_MODEL), 1.0),
        "p": nrm(ks[1], (DEPTH, BATCH, SEQ, PLE_DIM), 1.0),
        "norm1_g": gain(ks[2], (DEPTH, D_MODEL)),
        "w_in": nrm(ks[3], (DEPTH, D_MODEL, D_IN_PROJ), D_MODEL ** -0.5),
        "conv_w": nrm(ks[4], (DEPTH, CONV_WIDTH, CONV_W_2), CONV_WIDTH ** -0.5),
        "q_norm_g": gain(ks[5], (DEPTH, HEAD_DIM)),
        "k_norm_g": gain(ks[6], (DEPTH, HEAD_DIM)),
        "sgu_norm_g": gain(ks[7], (DEPTH, SGU_W)),
        "sgu_w": nrm(ks[8], (DEPTH, SGU_HEADS, CHUNK_2, CHUNK_2), CHUNK_2 ** -0.5),
        "sgu_b": gain(ks[9], (DEPTH, SGU_HEADS, CHUNK_2)),
        "w_out": nrm(ks[10], (DEPTH, D_MIX, D_MODEL), D_MIX ** -0.5),
        "norm2_g": gain(ks[11], (DEPTH, D_MODEL)),
        "w_ff1": nrm(ks[12], (DEPTH, D_MODEL, D_FF_2), D_MODEL ** -0.5),
        "w_ff2": nrm(ks[13], (DEPTH, D_FF_2, D_MODEL), D_FF_2 ** -0.5),
        "norm3_g": gain(ks[14], (DEPTH, D_MODEL)),
        "w_ple_gate": nrm(ks[15], (DEPTH, D_MODEL, D_MODEL), D_MODEL ** -0.5),
        "w_ple_proj": nrm(ks[16], (DEPTH, PLE_DIM, D_MODEL), PLE_DIM ** -0.5),
    }

def second_block(x, p, norm1_g, w_in, conv_w, q_norm_g, k_norm_g, sgu_norm_g, sgu_w, sgu_b,
              w_out, norm2_g, w_ff1, w_ff2, norm3_g, w_ple_gate, w_ple_proj):
    bsz, s_len, _ = x.shape
    split_idx = list(np.cumsum([CONV_W_2, CONV_W_2, CONV_W_2, ATTN_W, ATTN_W, ATTN_W, SGU_W]))
    h = x
    for i in range(DEPTH):
        hn = rms_norm(h, norm1_g[i])
        proj = hn @ w_in[i]
        a_b, a_c, a_h, q, k, v, c_u, c_v = jnp.split(proj, split_idx, axis=-1)
        y_a = a_b * short_conv(a_c * a_h, conv_w[i])
        q = rms_norm(q.reshape(bsz, s_len, ATTN_HEADS, HEAD_DIM), q_norm_g[i])
        k = rms_norm(k.reshape(bsz, s_len, ATTN_HEADS, HEAD_DIM), k_norm_g[i])
        v = v.reshape(bsz, s_len, ATTN_HEADS, HEAD_DIM)
        y_b = stick_breaking_attention(q, k, v).reshape(bsz, s_len, ATTN_W)
        y_c = spatial_gating(jax.nn.gelu(c_u, approximate=False),
                             jax.nn.gelu(c_v, approximate=False),
                             sgu_norm_g[i], sgu_w[i], sgu_b[i])
        h = h + jnp.concatenate([y_a, y_b, y_c], axis=-1) @ w_out[i]
        f = jnp.square(jax.nn.relu(rms_norm(h, norm2_g[i]) @ w_ff1[i]))
        h = h + f @ w_ff2[i]
        gate = jax.nn.sigmoid(rms_norm(h, norm3_g[i]) @ w_ple_gate[i])
        h = h + gate * (p[i] @ w_ple_proj[i])
    return h


def setup_inputs(seed=0):
    out = dict(first_inputs(seed))
    for name, value in second_inputs(seed + 1).items():
        if name != "x":
            out[name + "_2"] = value
    return out


def reference(
    x, norm_mix_g, norm_mlp_g, mlp_w1, mlp_w2, gdn_w_in, gdn_conv_w, gdn_a_log, gdn_dt_bias,
    gdn_o_norm_g, gdn_w_out, s5_w_in, s5_lam_re, s5_lam_im, s5_log_dt, s5_b_re, s5_b_im,
    s5_c_re, s5_c_im, s5_d, s5_w_out, m2_w_in, m2_conv_w, m2_conv_b, m2_dt_bias, m2_a_log, m2_d,
    m2_norm_g, m2_w_out, final_norm_g, p_2, norm1_g_2, w_in_2, conv_w_2, q_norm_g_2, k_norm_g_2,
    sgu_norm_g_2, sgu_w_2, sgu_b_2, w_out_2, norm2_g_2, w_ff1_2, w_ff2_2, norm3_g_2,
    w_ple_gate_2, w_ple_proj_2,
):
    x = first_block(
        x, norm_mix_g, norm_mlp_g, mlp_w1, mlp_w2, gdn_w_in, gdn_conv_w, gdn_a_log, gdn_dt_bias,
        gdn_o_norm_g, gdn_w_out, s5_w_in, s5_lam_re, s5_lam_im, s5_log_dt, s5_b_re, s5_b_im,
        s5_c_re, s5_c_im, s5_d, s5_w_out, m2_w_in, m2_conv_w, m2_conv_b, m2_dt_bias, m2_a_log,
        m2_d, m2_norm_g, m2_w_out, final_norm_g,
    )
    return second_block(
        x, p_2, norm1_g_2, w_in_2, conv_w_2, q_norm_g_2, k_norm_g_2, sgu_norm_g_2, sgu_w_2,
        sgu_b_2, w_out_2, norm2_g_2, w_ff1_2, w_ff2_2, norm3_g_2, w_ple_gate_2, w_ple_proj_2,
    )


_drawn_inputs = setup_inputs


def setup_inputs(seed=0):
    import zlib

    import numpy as np

    out = dict(_drawn_inputs(seed))
    spreads = {}
    factors = {'norm_mlp_g': 2.73,
     'gdn_o_norm_g': 3.709,
     'q_norm_g_2': 5.472,
     'k_norm_g_2': 7.43,
     'sgu_norm_g_2': 6.456,
     'sgu_b_2': 4.743,
     'norm3_g_2': 35.703}
    for name, (base, spread) in spreads.items():
        noise = np.random.default_rng([zlib.crc32(name.encode()), seed]).standard_normal(out[name].shape)
        drawn = base * np.exp(spread * noise) if base else spread * noise
        out[name] = __import__('jax').numpy.asarray(drawn.astype(out[name].dtype))
    for name, factor in factors.items():
        out[name] = (out[name] * factor).astype(out[name].dtype)
    return out
```

```python
from contextlib import ExitStack

import numpy as np

import concourse.bass as bass
from concourse import mybir

ACT = mybir.ActivationFunctionType
ALU = mybir.AluOpType
F32 = mybir.dt.float32
F32R = mybir.dt.float32r
BF16 = mybir.dt.bfloat16

P = 128
T = 512
D = 1024
KT = D // P
H = 8
C = T // P
EPS = 1e-6
LEVELS = 7
FF_GROUPS = 4
PAIRS = 4
TAPS = 4
HD = 64
TAPS2 = 3
LN_EXP = "natural_log_exp_and_others"
NEG = -1e30

U_OUT1 = 4 * H
U_FF1 = U_OUT1 + KT
U_PLE = U_FF1 + 16 * FF_GROUPS
U_ATT = U_PLE + 2
U_CONV = U_ATT + 4 * PAIRS
U_OUT2 = U_CONV + 6
U_FF2 = U_OUT2 + KT
U_GATE = U_FF2 + 16 * FF_GROUPS
U_END = U_GATE + KT

PC = {}
_n = 0
for _name, _width in (("mix_g", 8), ("mlp_g", 8), ("fin_g", 8), ("n1_g", 8), ("n2_g", 8), ("n3_g", 8),
                      ("conv_w", 96), ("conv2_w", 6), ("onorm_g", 1), ("q_g", 1), ("k_g", 1),
                      ("sgu_g", 2), ("a_log", 8), ("dt_b", 8)):
    PC[_name] = (_n, _n + _width)
    _n += _width
NPAR = _n

ZAT = ((0, 0, 0), (1, 0, T), (2, 0, 2 * T), (1, 3 * P, T + 3 * P))
ZBANK = ((0, T), (T, T), (2 * T, 2 * P))
ZW = 2 * T + 2 * P

CST = 1280


class Unit:

    def __init__(self, const, reg=0, per=0):
        if isinstance(reg, int):
            const, reg, per = const + reg * per, 0, 0
        assert per % 4 == 0
        self.const, self.reg, self.per = const, reg, per

    def plus(self, n):
        return Unit(self.const + n, self.reg, self.per)

    def number(self, n=0):
        return self.const + n if self.per == 0 else self.reg * self.per + (self.const + n)

    def half(self, n=0):
        return self.const // 2 + n if self.per == 0 else self.reg * (self.per // 2) + (self.const // 2 + n)

    def known_below(self, n):
        return self.per == 0 and self.const < n


def build(nc, a, out):
    ctx = ExitStack()
    with ctx:
        def sb(name, shape, dt=F32):
            return ctx.enter_context(nc.sbuf_tensor(name, shape, dt))

        def bank(name):
            return ctx.enter_context(nc.psum_tensor(name, [P, T], F32))

        def sem(name):
            return ctx.enter_context(nc.semaphore(name))

        h = sb("h", [P, KT, T])
        xh, xl = sb("xh", [P, KT, T], F32R), sb("xl", [P, KT, T], F32R)
        yh, yl = sb("yh", [P, KT, T], F32R), sb("yl", [P, KT, T], F32R)
        raw = [sb(f"raw{n}", [P, D]) for n in range(2)]
        wh = [sb(f"wh{n}", [P, D], F32R) for n in range(4)]
        wl = [sb(f"wl{n}", [P, D], F32R) for n in range(4)]
        cst = sb("cst", [P, CST])
        keep = sb("kept", [P, 3 * P])
        par = sb("par", [P, NPAR + KT + 1])
        xpad = sb("xpad", [P, T + 4])
        work = sb("work", [P, 29 * T])
        ident, ones, tri = keep[:, 0:P], keep[:, P:2 * P], keep[:, 2 * P:3 * P]

        def W(n, m=1):
            return work[:, n * T:(n + m) * T]

        def ch(ap, c):
            return ap[:, c * P:(c + 1) * P]

        def c3(ap):
            return ap.rearrange("p (c t) -> p c t", c=C)

        def ch5(ap, n):
            return ap[:, n * T:(n + 1) * T]

        def over_chunks(m):
            return m.unsqueeze(1).broadcast_to([P, C, P])

        def pc(name, n=0):
            lo = {"fn_g": NPAR, "q_g8": NPAR + KT}.get(name) or PC[name][0]
            return par[:, lo + n:lo + n + 1]

        kc, qc, vc, sk, sq = W(0), W(1), W(2), W(3), W(4)
        kT, qT, graw, gs, grow, brow = W(5), W(6), W(7), W(8), W(9), W(10)
        dec, Lt, qkd, Mb = W(11), W(12), W(13), [W(14), W(15)]
        Ti, TT, Xs, kb, kd, vb = W(16), W(17), W(18), W(19), W(20), W(21)
        nw, qd, vn, eg, osq, yb = W(22), W(23), W(24), W(25), W(26), W(27)
        S = W(28)[:, 0:P]
        tabs = W(28)[:, 128:288]
        tab5 = tabs.rearrange("p (x h) -> p x h", h=H)
        tcur = W(28)[:, 288:308]
        cwc = W(28)[:, 308:320]
        small = W(28)[:, 320:512]
        cwall = par[:, PC["conv_w"][0]:PC["conv_w"][1]].rearrange("p (x h) -> p x h", h=H)

        acc = [bank(f"acc{n}") for n in range(2)]
        ps = [bank(f"ps{n}") for n in range(6)]

        proj = nc.dram_tensor("proj", (P, KT, T), F32, kind="Internal").ap()
        rows = nc.dram_tensor("rows", (2, C, H, P), F32, kind="Internal").ap()

        s_par, s_x, s_cst, s_wab = sem("params_in"), [sem("x_in0"), sem("x_in1")], sem("const_in"), sem("wab_in")
        w_in = [sem(f"weights_in{n}") for n in range(2)]
        hi_done, lo_done, unit_done = sem("hi_done"), sem("lo_done"), sem("unit_done")
        evac = [sem(f"acc_evacuated{n}") for n in range(2)]
        sqs, accs_t, rs_mm, lnd, rst = sem("squares"), sem("sq_sums"), sem("rstd_mm"), sem("ln_done"), sem("rstd_ready")
        hn_done, xh_done, xl_done = sem("hn_done"), sem("xh_done"), sem("xl_done")
        g_act, g_dve, g_pe, g_dma = sem("gate_act"), sem("gate_dve"), sem("gate_pe"), sem("gate_rows_out")
        rows_in, cur_done, conv_st = sem("rows_in"), sem("cur_done"), sem("conv_steps")
        silu_d, ksq_d, kss_mm, kln, krs, kqn = (sem("silu_done"), sem("kq_squared"), sem("kq_sums"), sem("kq_ln"),
                                               sem("kq_rstd"), sem("kq_normed"))
        kk_d, qk_d, ktr_d, vtr_d = sem("kk_done"), sem("qk_done"), sem("k_transposed"), sem("v_transposed")
        darg_d, dec_d, dm_d, eg_d = sem("decay_arg"), sem("decay_exp"), sem("decay_masked"), sem("eg_done")
        lt1_d, lt_d, qkd_d, ktok_d, vb_d, qd_d = (sem("lt_half"), sem("lt_done"), sem("qkd_done"), sem("kbkd_done"),
                                                  sem("vb_done"), sem("qd_done"))
        m_d, l1_d, t_d, tt_d, x_d, xs_d, tx_d, xt_d = (sem("m_done"), sem("m1_transposed"), sem("t_updated"),
                                                       sem("tt_updated"), sem("x_done"), sem("x_copied"),
                                                       sem("tx_done"), sem("xt_done"))
        w_d, nw_d, v_d, vn_d, su_d, s_d, o_d = (sem("w_done"), sem("nw_done"), sem("v_done"), sem("vn_done"),
                                                sem("state_mm"), sem("s_done"), sem("o_done"))
        osq_d, oss_d, oln, ors, o1_d, yb_d, yh_d, yl_d = (sem("o_squared"), sem("o_sums"), sem("o_ln"), sem("o_rstd"),
                                                   sem("o_scaled"), sem("y_done"), sem("yh_done"), sem("yl_done"))
        out_d = sem("out_stored")
        zp = sem("zero_pad")
        m0_d = sem("m0_done")
        y_free = sem("yh_read")
        sqs2, sums2, rs2_mm, ln2, rs2 = (sem("squares2"), sem("sq_sums2"), sem("rstd2_mm"), sem("ln2_done"),
                                         sem("rstd2_ready"))
        scale_d, h_scaled = sem("token_scale"), sem("stream_scaled")
        vt_mm, vt_d, z_d, abs_d, ez_d, lz_d, sp_d = (sem("v2_transposed"), sem("v2_copied"), sem("scores_ready"),
                                                    sem("abs_scores"), sem("exp_scores"), sem("ln_scores"),
                                                    sem("softplus_done"))
        lw_d, aw_d, av_d, ao_d, ah_d, al_d = (sem("log_weights"), sem("weights_ready"), sem("attended"),
                                              sem("attended_copied"), sem("attended_hi"), sem("attended_lo"))
        qk_sq, qk_sum, qk_ln, qk_rs, qk_n = (sem("qk2_squared"), sem("qk2_sums"), sem("qk2_ln"), sem("qk2_rstd"),
                                             sem("qk2_normed"))
        cv, y_hi, y_lo = sem("conv2_steps"), sem("y2_hi"), sem("y2_lo")
        gelu_d, sg_sq, sg_sum, sg_ln, sg_rs, sg_n, sg_tr, sg_w, sg_mm, sg_b, sg_y = (
            sem("gelu_done"), sem("sgu_squared"), sem("sgu_sums"), sem("sgu_ln"), sem("sgu_rstd"), sem("sgu_normed"),
            sem("sgu_transposed"), sem("sgu_masked"), sem("sgu_mm"), sem("sgu_biased"), sem("sgu_y"))
        p_in, p_hi, p_lo, ple_mm, ple_cp = sem("p_in"), sem("p_hi"), sem("p_lo"), sem("ple_tiles"), sem("ple_copied")
        pp_out, pp_in = [sem("proj_out0"), sem("proj_out1")], sem("proj_in")
        gate_z, gate_s, gate_p, h_final = sem("gate_z"), sem("gate_sigmoid"), sem("gated"), sem("h_final")

        qr, kr, qs, ks = W(0), W(1), W(2), W(3)
        qn, kn, vr, vt = W(4), W(5), W(6), W(7)
        uv = W(8, 4)
        az, spz, aw = W(12, 3)[:, 0:ZW], W(15, 3)[:, 0:ZW], W(18, 3)[:, 0:ZW]
        ob, tscale = W(21), W(22)
        conv_in = [W(23 + n) for n in range(6)]
        sq2, sum2, rf, r1 = W(20), W(19), W(18), W(17)
        ph, pl = yh[:, 0:2, :], yl[:, 0:2, :]
        praw = W(12, 2).rearrange("p (k t) -> p k t", k=2)
        stage = [W(8, 4), W(12, 4)]
        pp = W(4, 8)
        pp3 = pp.rearrange("p (k t) -> p k t", t=T)
        gz = [W(14), W(15)]
        vtok, sgy = [W(12), W(13)], [W(14), W(15)]
        sg_cp = [sem("sgu_v_copied0"), sem("sgu_v_copied1")]
        ntri, nones, negm, blk = (ch(cst, n) for n in range(4))
        wsT, bsT = cst[:, 4 * P:8 * P], cst[:, 8 * P:10 * P]

        block = ctx.enter_context(nc.Block())

        def exists(u):
            return u.per != 0 or u.const < U_END

        def load_unit(sp, n, b):
            if not isinstance(n, int) or n >= 2:
                sp.wait_ge(lo_done, n - 1)
            sp.dma_start(raw[b][:].unsqueeze(1), a["weights"][:, bass.ds(n, 1), :]).then_inc(w_in[b], 16)

        def load_units(sp, first, last):
            with sp.Fori(first // 2, last // 2) as n:
                for b in range(2):
                    load_unit(sp, n * 2 + b, b)

        def split_hi(act, u):
            act.wait_ge(w_in[u.const % 2], u.half(1) * 16)
            if not u.known_below(4):
                act.wait_ge(unit_done, u.number(-3))
            nc.scalar.activation(wh[u.const % 4][:], raw[u.const % 2][:], ACT.Copy).then_inc(hi_done, 1)

        def split_lo(dve, u):
            dve.wait_ge(hi_done, u.number(1))
            if not u.known_below(4):
                dve.wait_ge(unit_done, u.number(-3))
            nc.vector.tensor_tensor(wl[u.const % 4][:], raw[u.const % 2][:], wh[u.const % 4][:].bitcast(F32),
                                    ALU.subtract).then_inc(lo_done, 1)

        def unit_steps(pe, u, mh, ml, gate=None, order=range(KT), freed=None):
            b, s = u.const % 2, u.const % 4
            pe.wait_ge(lo_done, u.number(1))
            if not u.known_below(2):
                pe.wait_ge(evac[b], u.half())
            for n, k in enumerate(order):
                if gate is not None:
                    gate(k)
                hi, lo = ch(wh[s], k), ch(wl[s], k)
                nc.tensor.matmul(acc[b][:], hi, mh[:, k, :], start=(n == 0), stop=False)
                nc.tensor.matmul(acc[b][:], hi, ml[:, k, :], start=False, stop=False)
                mm = nc.tensor.matmul(acc[b][:], lo, mh[:, k, :], start=False, stop=(n == KT - 1))
                if n == KT - 1:
                    mm.then_inc(unit_done, 1)
                elif n == 1 and freed is not None:
                    mm.then_inc(freed, 1)
                yield

        def run_unit(pe, u, mh, ml, gate=None, order=range(KT), freed=None):
            for _ in unit_steps(pe, u, mh, ml, gate, order, freed):
                pass

        @block.sync
        def _(sp):
            sp.dma_start(par[:, 0:NPAR], a["params"]).then_inc(s_par, 16)
            for half in range(2):
                sp.dma_start(h[:, 4 * half:4 * half + 4, :],
                             a["xT"].rearrange("(k p) t -> p k t", p=P)[:, 4 * half:4 * half + 4, :]).then_inc(s_x[half], 16)
            sp.dma_start(keep[:], a["keep"]).then_inc(s_par, 16)
            sp.dma_start(W(21)[:, 0:P], a["w_ab"]).then_inc(s_wab, 16)
            for n in range(2):
                load_unit(sp, n, n)
            sp.dma_start(cst[:, 0:LEVELS * P], a["levels"]).then_inc(s_cst, 16)
            load_units(sp, 2, U_OUT1 + 2)
            sp.wait_ge(m0_d, H)
            sp.wait_ge(m_d, H * (LEVELS - 1))
            sp.dma_start(cst[:], a["cst2"]).then_inc(s_cst, 16)
            load_units(sp, U_OUT1 + 2, U_FF1)
            sp.wait_ge(o_d, H)
            sp.dma_start(praw, a["pT"].rearrange("(k p) t -> p k t", p=P)).then_inc(p_in, 16)
            load_units(sp, U_FF1, U_FF2)
            sp.wait_ge(y_lo, 4)
            for n in range(2):
                sp.wait_ge(pp_out[n], 16)
                sp.dma_start(pp3[:, 4 * n:4 * n + 4, :], proj[:, 4 * n:4 * n + 4, :]).then_inc(pp_in, 16)
            load_units(sp, U_FF2, U_END)
            for m in range(KT):
                sp.wait_ge(h_final, m + 1)
                sp.dma_start(out[m * P:(m + 1) * P, :], h[:, m, :]).then_inc(out_d, 16)
            sp.wait_ge(out_d, 16 * KT)

        def pe_gate_steps(pe):
            def mm():
                pe.wait_ge(g_dve, 1)
                for k in range(KT):
                    hi, lo = wh[3][:, k * 16:(k + 1) * 16], wl[3][:, k * 16:(k + 1) * 16]
                    nc.tensor.matmul(ps[1][0:16, :], hi, xh[:, k, :], start=(k == 0), stop=False)
                    nc.tensor.matmul(ps[1][0:16, :], hi, xl[:, k, :], start=False, stop=False)
                    last = nc.tensor.matmul(ps[1][0:16, :], lo, xh[:, k, :], start=False, stop=(k == KT - 1))
                last.then_inc(g_pe, 1)

            def tr():
                pe.wait_ge(g_dve, 2)
                for c in range(C):
                    last = nc.tensor.transpose(ps[2][:, c * 16:(c + 1) * 16], ch(W(22), c)[0:16, :], ident[0:16, 0:16])
                last.then_inc(g_pe, 1)

            def cum():
                pe.wait_ge(g_dve, 5)
                nc.tensor.matmul(ps[3][:, 0:32], tri, small[:, 96:128], start=True, stop=True)
                nc.tensor.matmul(ps[3][:, 32:64], ones, small[:, 96:128], start=True, stop=True).then_inc(g_pe, 1)

            def row():
                pe.wait_ge(g_dve, 8)
                nc.tensor.transpose(ps[4][0:64, 0:P], tabs[:, 0:64], ident).then_inc(g_pe, 1)

            return [mm, tr, cum, row]

        def pe_head_steps(pe, i):
            b = i - 1

            def first():
                pe.wait_ge(kqn, i * 2 - 1)
                for c in range(C):
                    last = nc.tensor.matmul(ch(ps[0], c), ch(kT, c), ch(kT, c), start=True, stop=True)
                last.then_inc(kk_d, 1)
                pe.wait_ge(kqn, i * 2)
                for c in range(C):
                    last = nc.tensor.matmul(ch(ps[1], c), ch(kT, c), ch(qT, c), start=True, stop=True)
                last.then_inc(qk_d, 1)
                for c in range(C):
                    last = nc.tensor.transpose(ch(ps[2], c), ch(kT, c), ident)
                last.then_inc(ktr_d, 1)
                pe.wait_ge(silu_d, i * 4 - 1)
                for c in range(C):
                    last = nc.tensor.transpose(ch(ps[3], c), ch(vc, c), ident)
                last.then_inc(vtr_d, 1)

            def level1():
                pe.wait_ge(m0_d, i)
                if not isinstance(i, int) or i > 1:
                    pe.wait_ge(oln, b)
                for c in range(C):
                    last = nc.tensor.transpose(ch(ps[4], c), ch(Mb[0], c), ident)
                last.then_inc(l1_d, 1)

            def x(n):
                def step():
                    pe.wait_ge(m_d, b * 6 + n)
                    pe.wait_ge(t_d, b * 6 + n)
                    for c in range(C):
                        last = nc.tensor.matmul(ch(ps[0], c), ch(Mb[n % 2], c), ch(Ti, c), start=True, stop=True)
                    last.then_inc(x_d, 1)
                return step

            def tx(n):
                def step():
                    pe.wait_ge(xs_d, b * 6 + n)
                    pe.wait_ge(tt_d, b * LEVELS + n)
                    if n == 1:
                        pe.wait_ge(qkd_d, i)
                        pe.wait_ge(ktok_d, i)
                    if n < 6:
                        for c in range(C):
                            last = nc.tensor.matmul(ch(ps[1], c), ch(TT, c), ch(Xs, c), start=True, stop=True)
                        last.then_inc(tx_d, 1)
                    for c in range(C):
                        last = nc.tensor.matmul(ch(ps[2], c), ch(Xs, c), ch(TT, c), start=True, stop=True)
                    last.then_inc(xt_d, 1)
                return step

            def w():
                pe.wait_ge(tt_d, i * LEVELS)
                for c in range(C):
                    last = nc.tensor.matmul(ch(ps[1], c), ch(kb, c), ch(TT, c), start=True, stop=True)
                last.then_inc(w_d, 1)

            def v(c):
                def step():
                    if c == 0:
                        pe.wait_ge(vb_d, i)
                    nc_ = nc.tensor
                    last = nc_.matmul(ch(ps[3], c), ch(TT, c), ch(vb, c), start=True, stop=(c == 0))
                    if c > 0:
                        if c == 1:
                            pe.wait_ge(nw_d, i)
                        pe.wait_ge(s_d, b * 3 + c)
                        last = nc_.matmul(ch(ps[3], c), ch(nw, c), S, start=False, stop=True)
                    last.then_inc(v_d, 1)
                    if c > 0:
                        if c == 1:
                            pe.wait_ge(qd_d, i)
                        nc_.matmul(ch(ps[5], c), S, ch(qd, c), start=True, stop=False)
                return step

            def os(c):
                def step():
                    pe.wait_ge(vn_d, b * 4 + c + 1)
                    if c < C - 1:
                        nc.tensor.matmul(ps[4][:, 0:P], ch(kd, c), ch(vn, c), start=True, stop=True).then_inc(su_d, 1)
                    if c == 0 and (not isinstance(i, int) or i > 1):
                        pe.wait_ge(o1_d, b)
                    last = nc.tensor.matmul(ch(ps[5], c), ch(vn, c), ch(qkd, c), start=(c == 0), stop=True)
                    if c == C - 1:
                        last.then_inc(o_d, 1)
                return step

            def norm():
                pe.wait_ge(osq_d, i)
                nc.tensor.matmul(ps[4][:], ones, osq, start=True, stop=True).then_inc(oss_d, 1)

            return ([first, level1] + [s for n in range(1, 7) for s in (x(n), tx(n))]
                    + [w] + [s for c in range(C) for s in (v(c), os(c))] + [norm])

        def pe_kq_norm(pe, i, n):
            if n == 0 and (not isinstance(i, int) or i > 0):
                pe.wait_ge(nw_d, i)
                pe.wait_ge(tt_d, i * LEVELS)
            pe.wait_ge(ksq_d, i * 2 + n + 1)
            nc.tensor.matmul(ps[1 + n][:], ones, (sk, sq)[n], start=True, stop=True).then_inc(kss_mm, 1)

        FILL = [4, 2, 2, 1, 2, 1, 2, 1, 2, 1, 2, 1, 2, 1, 0, 1, 1, 0, 1, 0, 1, 0, 2, 2]
        KQ_AT = {18: 0, 19: 1}
        assert sum(FILL) == 4 * KT
        LAST_FILL = [3, 2, 1, 0, 1, 0, 1, 0, 1, 0, 1, 0, 1, 1, 0, 0, 0, 0, 0, 0, 0, 0, 1, 1]
        assert sum(LAST_FILL) == 2 * (KT - 1)

        def pe_out_steps(pe):
            firsts = [unit_steps(pe, Unit(U_OUT1 + n), yh, yl) for n in range(2)]
            pe.wait_ge(yl_d, H - 2)
            for unit in firsts:
                for _ in range(KT - 2):
                    next(unit)
                    yield
            pe.wait_ge(yl_d, H - 1)
            for unit in firsts:
                next(unit)
                yield
            pe.wait_ge(yl_d, H)
            for unit in firsts:
                for _ in unit:
                    pass
            yield

        def pe_gdn(pe, i, head, project, out_steps=None):
            def units():
                for n in range(4):
                    yield from unit_steps(pe, Unit(n, i, 4), xh, xl)
            todo = units()
            if head:
                for at, step in enumerate(pe_head_steps(pe, i)):
                    step()
                    if project:
                        for _ in range(FILL[at]):
                            next(todo)
                        if at in KQ_AT:
                            pe_kq_norm(pe, i, KQ_AT[at])
                    else:
                        for _ in range(LAST_FILL[at]):
                            next(out_steps)
            else:
                gates = pe_gate_steps(pe)
                for n in range(4 * KT):
                    if n % KT == 0:
                        gates[n // KT]()
                    next(todo)
                    if n == 4 * KT - 2:
                        pe_kq_norm(pe, i, 0)
                        pe_kq_norm(pe, i, 1)
            if project:
                for _ in todo:
                    pass

        def pe_mlp(pe, base, g, x0, first, freed=None):
            for n in range(KT):
                u = Unit(base + n, g, 16)
                if first and n == 0:
                    def gate(k):
                        pe.wait_ge(xl_done, x0 + k + 1)
                    run_unit(pe, u, xh, xl, gate)
                    rstd_mm(pe, x0 + KT)
                else:
                    run_unit(pe, u, xh, xl)
            for n in range(KT):
                u = Unit(base + KT + n, g, 16)
                gate = None
                if n == 0:
                    def gate(k):
                        pe.wait_ge(yl_done, hid_count(base, g) + k + 1)
                run_unit(pe, u, yh, yl, gate, freed=freed if n == KT - 1 else None)

        def hid_count(base, g):
            return (0 if base == U_FF1 else FF_GROUPS * KT) + g * KT

        def rstd_mm(pe, sums):
            pe.wait_ge(accs_t, sums)
            nc.tensor.matmul(ps[0][:], ones, accb, start=True, stop=True).then_inc(rs_mm, 1)

        accb, rstd = W(27), W(28)
        yl_done = sem("hidden_split")
        hid_sq, hid_h = sem("hidden_squared"), sem("hidden_hi")

        def pe_pair_steps(pe, i):
            b = i - 1
            past = not isinstance(i, int) or i > 1

            def vtok():
                u = Unit(U_ATT - 4 + 2, i, 4)
                pe.wait_ge(evac[u.const % 2], u.half(1))
                pe.wait_ge(qk_ln, i * 2)
                for c in range(C):
                    last = nc.tensor.transpose(ch(ps[4], c), ch(vr, c), ident)
                last.then_inc(vt_mm, 1)

            def scores(n):
                rows_ = slice(HD * n, HD * (n + 1))

                def step():
                    if n == 0:
                        pe.wait_ge(qk_n, i * 2)
                    if n > 0 or past:
                        pe.wait_ge(aw_d, b * 2 + n)
                    for kb, (z, at, _) in enumerate(ZAT):
                        nc.tensor.matmul(ps[z][:, at:at + T - kb * P], ch(kn, kb)[rows_, :], qn[rows_, kb * P:],
                                         start=(kb < 3), stop=False, skip_group_check=True)
                    for kb, (z, at, _) in enumerate(ZAT):
                        last = nc.tensor.matmul(ps[z][:, at:at + P], ident, negm, start=False, stop=False,
                                                skip_group_check=True)
                    last.then_inc(z_d, 1)
                return step

            def suffix(n):
                def step():
                    pe.wait_ge(sp_d, b * 2 + n + 1)
                    for kb, (z, at, _) in enumerate(ZAT):
                        for k2 in range(kb, C):
                            at2, w2 = ZAT[k2][2], T - k2 * P
                            last = nc.tensor.matmul(ps[z][:, at + (k2 - kb) * P:at + T - kb * P],
                                                    ntri if k2 == kb else nones, spz[:, at2:at2 + w2],
                                                    start=False, stop=(k2 == C - 1), skip_group_check=True)
                    last.then_inc(lw_d, 1)
                return step

            def attend(n):
                def step():
                    pe.wait_ge(aw_d, b * 2 + n + 1)
                    if n == 0:
                        pe.wait_ge(vt_d, i)
                        if past:
                            pe.wait_ge(al_d, b)
                    for kb, (_, _, at) in enumerate(ZAT):
                        last = nc.tensor.matmul(ps[3][HD * n:HD * (n + 1), kb * P:], ch(vt, kb)[:, HD * n:HD * (n + 1)],
                                                aw[:, at:at + T - kb * P], start=(kb == 0), stop=(kb == C - 1))
                    last.then_inc(av_d, 1)
                return step

            return [vtok, scores(0), suffix(0), attend(0), scores(1), suffix(1), attend(1)]

        def pe_qk_sum(pe, i, n):
            pe.wait_ge(qk_sq, i * 2 + n + 1)
            if not isinstance(i, int) or i > 0:
                pe.wait_ge(qk_ln, i * 2)
                pe.wait_ge(vt_d, i)
            nc.tensor.matmul(ps[5 - n][:], blk, (qs, ks)[n], start=True, stop=True).then_inc(qk_sum, 1)

        def pe_proj(pe, n):
            u = U_PLE + n
            pe.wait_ge(lo_done, u + 1)
            if n == 0:
                pe.wait_ge(p_lo, 1)
            else:
                pe.wait_ge(evac[(u - 1) % 2], (u - 1) // 2 + 1)
            for m in range(4):
                for k in range(2):
                    hi, lo = ch(wh[u % 4], k * 4 + m), ch(wl[u % 4], k * 4 + m)
                    nc.tensor.matmul(ps[2 + m][:], hi, ph[:, k, :], start=(k == 0), stop=False)
                    nc.tensor.matmul(ps[2 + m][:], hi, pl[:, k, :], start=False, stop=False)
                    mm = nc.tensor.matmul(ps[2 + m][:], lo, ph[:, k, :], start=False, stop=(k == 1))
                mm.then_inc(unit_done if m == 3 else ple_mm, 1)

        ATT_FILL = [0, 8, 4, 0, 8, 4, 8]

        def pe_att(pe, i, head, project):
            normed = not (isinstance(i, int) and i == PAIRS)
            if not head:
                pe.wait_ge(s_cst, 32)

                def gate(k):
                    pe.wait_ge(xl_done, 2 * KT + k + 1)
                pe_proj(pe, 0)
                pe.wait_ge(accs_t, 3 * KT)
                nc.tensor.matmul(ps[0][:], ones, accb, start=True, stop=True).then_inc(rs2_mm, 1)
                pe.wait_ge(sums2, KT)
                nc.tensor.matmul(ps[1][:], ones, sum2, start=True, stop=True).then_inc(rs2_mm, 1)
                pe_proj(pe, 1)
                run_unit(pe, Unit(U_ATT), xh, xl, gate)
                run_unit(pe, Unit(U_ATT + 1), xh, xl)
                run_unit(pe, Unit(U_ATT + 2), xh, xl)
                pe_qk_sum(pe, i, 0)
                pe_qk_sum(pe, i, 1)
                run_unit(pe, Unit(U_ATT + 3), xh, xl)
                return

            def units():
                for n in range(4):
                    yield from unit_steps(pe, Unit(U_ATT + n, i, 4), xh, xl)
            todo, done = units(), 0
            for at, step in enumerate(pe_pair_steps(pe, i)):
                step()
                for _ in range(ATT_FILL[at]):
                    next(todo)
                    done += 1
                    if normed and done in (16, 24):
                        pe_qk_sum(pe, i, done // 8 - 2)
            for _ in todo:
                pass

        def pe_conv_sgu(pe):
            for t in range(2):
                pe.wait_ge(sg_sq, t + 1)
                nc.tensor.matmul(ps[5 - t][:], blk, (qs, ks)[t], start=True, stop=True).then_inc(sg_sum, 1)
            run_unit(pe, Unit(U_CONV + 4), xh, xl)
            for t in range(2):
                pe.wait_ge(sg_n, t + 1)
                for c in range(C):
                    last = nc.tensor.transpose(ch(ps[t], c), ch((qn, kn)[t], c), ident)
                last.then_inc(sg_tr, 1)
            last_unit = unit_steps(pe, Unit(U_CONV + 5), xh, xl)
            for _ in range(KT // 2):
                next(last_unit)
            pe.wait_ge(al_d, PAIRS)
            pe.wait_ge(sg_w, 1)
            for t in range(2):
                pe.wait_ge(sg_cp[t], 1)
                for n in range(2):
                    for c in range(C):
                        last = nc.tensor.matmul(ps[2 + t][HD * n:HD * (n + 1), c * P:(c + 1) * P],
                                                ch(vtok[t], c)[:, HD * n:HD * (n + 1)], ch(wsT, 2 * t + n),
                                                start=True, stop=True)
                last.then_inc(sg_mm, 1)
            for _ in last_unit:
                pass

        def mixed_gate(k):
            if k < 2:
                nc.tensor.wait_ge(y_lo, (1, 4)[k])
            elif k == 2:
                nc.tensor.wait_ge(al_d, PAIRS)
            elif k >= 6:
                nc.tensor.wait_ge(y_lo, k - 4)

        def pe_final(pe):
            for n in range(KT):
                def gate(k):
                    pe.wait_ge(xl_done, 4 * KT + k + 1)
                run_unit(pe, Unit(U_GATE + n), xh, xl, gate if n == 0 else None)
                if n == 0:
                    rstd_mm(pe, 5 * KT)

        @block.tensor
        def _(pe):
            pe.wait_ge(s_par, 32)
            rstd_mm(pe, KT)
            pe.wait_ge(xl_done, KT)
            pe_gdn(pe, 0, False, True)
            pe_gdn(pe, 1, True, True)
            with pe.Fori(2, H) as i:
                pe_gdn(pe, i, True, True)
            out_steps = pe_out_steps(pe)
            pe_gdn(pe, H, True, False, out_steps)
            next(out_steps)
            for n in range(2, KT):
                run_unit(pe, Unit(U_OUT1 + n), yh, yl)
            pe_mlp(pe, U_FF1, 0, KT, True)
            with pe.Fori(1, FF_GROUPS - 1) as g:
                pe_mlp(pe, U_FF1, g, 0, False)
            pe_mlp(pe, U_FF1, FF_GROUPS - 1, 0, False, freed=y_free)
            pe_att(pe, 0, False, True)
            pe_att(pe, 1, True, True)
            with pe.Fori(2, PAIRS) as i:
                pe_att(pe, i, True, True)
            pe_att(pe, PAIRS, True, True)
            pe_conv_sgu(pe)
            order = (2, 3, 4, 5, 6, 7, 0, 1)
            firsts = [unit_steps(pe, Unit(U_OUT2 + n), yh, yl, mixed_gate, order) for n in range(2)]
            for unit in firsts:
                for _ in range(4):
                    next(unit)
            for unit in firsts:
                for _ in unit:
                    pass
            for n in range(2, KT):
                run_unit(pe, Unit(U_OUT2 + n), yh, yl)
            pe_mlp(pe, U_FF2, 0, 3 * KT, True)
            with pe.Fori(1, FF_GROUPS) as g:
                pe_mlp(pe, U_FF2, g, 0, False)
            pe_final(pe)

        def act_rstd(act, n, src, dst, scale, bias=0.0):
            act.wait_ge(rs_mm, n)
            nc.scalar.activation(dst, src, ACT.Ln, scale=scale, bias=EPS).then_inc(lnd, 1)
            act.wait_ge(lnd, n)
            nc.scalar.activation(dst, dst, ACT.Exp, scale=-0.5).then_inc(rst, 1)

        def act_silu(act, i, n, buf):
            nc.scalar.activation(buf, buf, ACT.Silu).then_inc(silu_d, 1)

        def act_gate_steps(act):
            def s1():
                act.wait_ge(g_dve, 4)
                nc.scalar.activation(small[:, 64:96], small[:, 0:32], ACT.Abs).then_inc(g_act, 1)
                act.wait_ge(g_act, 2)
                nc.scalar.activation(small[:, 64:96], small[:, 64:96], ACT.Exp, scale=-1.0).then_inc(g_act, 1)
                act.wait_ge(g_act, 3)
                nc.scalar.activation(small[:, 64:96], small[:, 64:96], ACT.Ln, bias=1.0).then_inc(g_act, 1)
                nc.scalar.activation(small[:, 128:160], small[:, 32:64], ACT.Exp, scale=-1.0).then_inc(g_act, 1)
                nc.scalar.activation(small[:, 160:168], par[:, PC["a_log"][0]:PC["a_log"][1]], ACT.Exp).then_inc(g_act, 1)

            def s2():
                act.wait_ge(g_dve, 8)
                nc.scalar.activation(tabs[:, 64:96], tabs[:, 0:32], ACT.Exp).then_inc(g_act, 1)
                nc.scalar.activation(tabs[:, 96:160], tabs[:, 96:160], ACT.Exp).then_inc(g_act, 1)

            def s3():
                act.wait_ge(g_dve, 10)
                act.dma_start(rows.rearrange("s c h t -> (s c h) t"), W(23)[0:64, 0:P]).then_inc(g_dma, 16)
            return s1, s2, s3

        def act_rows(act, i):
            for s, dst in ((0, grow), (1, brow)):
                src = rows[s][:, bass.ds(i, 1), :].rearrange("c a t -> (c a) t").partition_broadcast(P)
                act.dma_start(c3(dst), src).then_inc(rows_in, 16)

        def act_gdn(act, i, head, project):
            b = i - 1
            nonfirst = not isinstance(i, int) or i > 0

            def xcopy(n):
                act.wait_ge(x_d, b * 6 + n)
                if n > 1 or not isinstance(i, int) or i > 1:
                    act.wait_ge(xt_d, b * 6 + n - 1)
                nc.scalar.activation(Xs, ps[0][:], ACT.Copy).then_inc(xs_d, 1)

            def take(n, split=True):
                u = Unit(n, i, 4)
                if split:
                    split_hi(act, u.plus(2))
                act.wait_ge(unit_done, u.number(1))
                if n < 3:
                    if n > 0 or nonfirst:
                        act.wait_ge(conv_st, i * 12 + 4 * n)
                    else:
                        act.wait_ge(zp, 1)
                    nc.scalar.activation(xpad[:, 3:3 + T], acc[u.const % 2][:], ACT.Copy).then_inc(evac[u.const % 2], 1)
                else:
                    nc.scalar.activation(graw, acc[u.const % 2][:], ACT.Copy).then_inc(evac[u.const % 2], 1)

            if head:
                act.wait_ge(darg_d, i)
                nc.scalar.activation(dec, dec, ACT.Exp).then_inc(dec_d, 1)
                split_hi(act, Unit(1, i, 4))
                act.wait_ge(unit_done, Unit(-1, i, 4).number(1))
                nc.scalar.activation(graw, acc[1][:], ACT.Copy).then_inc(evac[1], 1)
                if not isinstance(i, int) or i > 1:
                    act.wait_ge(qd_d, b)
                act.wait_ge(rows_in, i * 32)
                nc.scalar.activation(eg, grow, ACT.Exp).then_inc(eg_d, 1)
                xcopy(1)
                if project:
                    take(0)
                xcopy(2)
                xcopy(3)
                if project:
                    take(1)
                xcopy(4)
                xcopy(5)
                if project:
                    split_hi(act, Unit(4, i, 4))
                xcopy(6)
                if project:
                    take(2, split=False)
                    act.wait_ge(lt_d, i)
                    act.wait_ge(eg_d, i)
                    act_rows(act, i)
            else:
                s1, s2, s3 = act_gate_steps(act)
                take(0)
                s1()
                take(1)
                s2()
                take(2)
                s3()
            if project:
                if head:
                    act_nw(act, i)
                    act_gs(act, i)
                act.wait_ge(conv_st, i * 12 + 4)
                nc.scalar.activation(kc, kc, ACT.Silu).then_inc(silu_d, 1)
                act.wait_ge(conv_st, i * 12 + 8)
                nc.scalar.activation(qc, qc, ACT.Silu).then_inc(silu_d, 1)
                act.wait_ge(silu_d, i * 4 + 2)
                nc.scalar.activation(sk, kc, ACT.Square).then_inc(ksq_d, 1)
                nc.scalar.activation(sq, qc, ACT.Square).then_inc(ksq_d, 1)
                act.wait_ge(conv_st, i * 12 + 12)
                nc.scalar.activation(vc, vc, ACT.Silu).then_inc(silu_d, 1)
            else:
                act_nw(act, i)
                act_gs(act, i)
            act.preload_act_table_set(LN_EXP)
            if project:
                for n, buf in enumerate((sk, sq)):
                    act.wait_ge(kss_mm, i * 2 + n + 1)
                    nc.scalar.activation(buf, ps[1 + n][:], ACT.Ln, bias=EPS).then_inc(kln, 1)
                for n, buf in enumerate((sk, sq)):
                    act.wait_ge(kln, i * 2 + n + 1)
                    nc.scalar.activation(buf, buf, ACT.Exp, scale=-0.5).then_inc(krs, 1)
                if not head:
                    act.wait_ge(g_dma, 16)
                    act_rows(act, i)
            if head:
                act.wait_ge(o_d, i)
                nc.scalar.activation(osq, ps[5][:], ACT.Square).then_inc(osq_d, 1)
                act.wait_ge(oss_d, i)
                nc.scalar.activation(osq, ps[4][:], ACT.Ln, scale=1.0 / P, bias=EPS).then_inc(oln, 1)
                act.wait_ge(oln, i)
                nc.scalar.activation(osq, osq, ACT.Exp, scale=-0.5).then_inc(ors, 1)
        def act_nw(act, i):
            act.wait_ge(w_d, i)
            nc.scalar.activation(nw, ps[1][:], ACT.Copy, scale=-1.0).then_inc(nw_d, 1)

        def act_gs(act, i):
            if not isinstance(i, int) or i > 1:
                act.wait_ge(yb_d, i - 1)
            act.wait_ge(evac[1], i * 2)
            nc.scalar.activation(gs, graw, ACT.Silu).then_inc(silu_d, 1)

        act_nrm = [KT]

        def act_norm_tile(act, m, b, half, gname):
            n = act_nrm[0]
            act_nrm[0] += 1
            act.wait_ge(evac[b], half)
            nc.scalar.activation(xh[:, m, :], h[:, m, :], ACT.Copy, scale=pc(gname, m)).then_inc(xh_done, 1)
            act.wait_ge(accs_t, n)
            nc.scalar.activation(W(26), h[:, m, :], ACT.Square).then_inc(sqs, 1)
            if gname == "fn_g":
                if m > 0:
                    act.wait_ge(sums2, m)
                nc.scalar.activation(sq2, h[:, m, :], ACT.Square, scale=pc("fin_g", m)).then_inc(sqs2, 1)

        def act_mlp(act, base, g, first, last, gname):
            for n in range(KT):
                u = Unit(base + n, g, 16)
                split_hi(act, u.plus(2))
                if first and n == 0:
                    act_rstd(act, 2 if base == U_FF1 else 3, ps[0][:], rstd, 1.0 / D)
                cnt = hid_count(base, g) + n
                act.wait_ge(evac[u.const % 2], u.half(1))
                if not isinstance(cnt, int) or cnt > 0:
                    act.wait_ge(yl_done, cnt)
                nc.scalar.activation(hs, hr, ACT.Square).then_inc(hid_sq, 1)
                act.wait_ge(hid_sq, cnt + 1)
                nc.scalar.activation(yh[:, n, :], hs, ACT.Copy).then_inc(hid_h, 1)
            for n in range(KT):
                u = Unit(base + KT + n, g, 16)
                if exists(u.plus(2)):
                    split_hi(act, u.plus(2))
                if last and base == U_FF1 and n == KT - 1:
                    act.wait_ge(p_in, 16)
                    act.wait_ge(y_free, 1)
                    nc.scalar.activation(ph, praw, ACT.Copy).then_inc(p_hi, 1)
                if last:
                    act_norm_tile(act, n, u.const % 2, u.half(1), gname)

        hr, hs = W(24), W(25)

        def act_rsqrt(act, buf, src, scale, summed, summed_n, ln_sem, rs_sem, n):
            act.wait_ge(summed, summed_n)
            nc.scalar.activation(buf, src, ACT.Ln, scale=scale, bias=EPS).then_inc(ln_sem, 1)
            act.wait_ge(ln_sem, n)
            nc.scalar.activation(buf, buf, ACT.Exp, scale=-0.5).then_inc(rs_sem, 1)

        def act_proj(act, n):
            u = U_PLE + n
            split_hi(act, Unit(u + 2))
            if n == 1:
                act.wait_ge(p_lo, 1)
            for m in range(4):
                if m < 3:
                    act.wait_ge(ple_mm, 3 * n + m + 1)
                else:
                    act.wait_ge(unit_done, u + 1)
                nc.scalar.activation(ch5(stage[n], m), ps[2 + m][:], ACT.Copy).then_inc(ple_cp if m < 3 else evac[u % 2], 1)
            act.wait_ge(ple_cp, 3 * n + 3)
            act.wait_ge(evac[u % 2], u // 2 + 1)
            act.dma_start(proj[:, 4 * n:4 * n + 4, :], stage[n].rearrange("p (k t) -> p k t", t=T)).then_inc(pp_out[n], 16)

        def act_att(act, i, head, project):
            b = i - 1
            past = not isinstance(i, int) or i > 1
            normed = not (isinstance(i, int) and i == PAIRS)

            def hi(n):
                split_hi(act, Unit(U_ATT + n + 2, i, 4))

            def soft(n):
                act.wait_ge(z_d, b * 2 + n + 1)
                if n > 0 or past:
                    act.wait_ge(sp_d, b * 2 + n)
                for z, (at, w) in enumerate(ZBANK):
                    last = nc.scalar.activation(az[:, at:at + w], ps[z][:, 0:w], ACT.Abs)
                last.then_inc(abs_d, 1)
                act.wait_ge(abs_d, b * 2 + n + 1)
                nc.scalar.activation(az, az, ACT.Exp, scale=-1.0).then_inc(ez_d, 1)
                act.wait_ge(ez_d, b * 2 + n + 1)
                nc.scalar.activation(az, az, ACT.Ln, bias=1.0).then_inc(lz_d, 1)

            def weights(n):
                act.wait_ge(lw_d, b * 2 + n + 1)
                if n > 0 or past:
                    act.wait_ge(av_d, b * 2 + n)
                for z, (at, w) in enumerate(ZBANK):
                    last = nc.scalar.activation(aw[:, at:at + w], ps[z][:, 0:w], ACT.Exp)
                last.then_inc(aw_d, 1)

            def square(n):
                u = Unit(U_ATT + n, i, 4)
                act.wait_ge(evac[u.const % 2], u.half(1))
                if head:
                    act.wait_ge(qk_n, i * 2)
                nc.scalar.activation((qs, ks)[n], (qr, kr)[n], ACT.Square).then_inc(qk_sq, 1)

            def rsqrt(n):
                act_rsqrt(act, (qs, ks)[n], ps[5 - n][:], 1.0 / HD, qk_sum, i * 2 + n + 1, qk_ln, qk_rs, i * 2 + n + 1)

            if not head:
                act_proj(act, 0)
                act_rsqrt(act, rf, ps[0][:], 1.0 / D, rs2_mm, 1, ln2, rs2, 1)
                act_proj(act, 1)
                hi(0)
                act_rsqrt(act, r1, r1, 1.0 / D, scale_d, 2, ln2, rs2, 2)
                hi(1)
                square(0)
                square(1)
                hi(2)
                rsqrt(0)
                rsqrt(1)
                hi(3)
                act.wait_ge(pp_out[1], 16)
                return
            hi(0)
            act.wait_ge(vt_mm, i)
            if past:
                act.wait_ge(av_d, b * 2)
            nc.scalar.activation(vt, ps[4][:], ACT.Copy).then_inc(vt_d, 1)
            soft(0)
            hi(1)
            weights(0)
            if normed:
                square(0)
            soft(1)
            if normed:
                square(1)
                rsqrt(0)
            hi(2)
            weights(1)
            if normed:
                rsqrt(1)
            hi(3)

        def act_conv_sgu(act):
            for t in range(4):
                u = U_ATT + 4 * PAIRS - 1
                act.wait_ge(evac[u % 2], u // 2 + 1)
                nc.scalar.activation(ch5(uv, t), ch5(uv, t), ACT.Gelu).then_inc(gelu_d, 1)
            for t in range(2):
                act.wait_ge(gelu_d, 3 + t)
                nc.scalar.activation((qs, ks)[t], ch5(uv, 2 + t), ACT.Square).then_inc(sg_sq, 1)
            split_hi(act, Unit(U_CONV + 6))
            act.preload_act_table_set(LN_EXP)
            for t in range(2):
                act_rsqrt(act, (qs, ks)[t], ps[5 - t][:], 1.0 / HD, sg_sum, t + 1, sg_ln, sg_rs, t + 1)
            act.wait_ge(cv, 5)
            nc.scalar.activation(yh[:, 0, :], qr, ACT.Copy).then_inc(y_hi, 1)
            act.wait_ge(sg_tr, 1)
            nc.scalar.activation(vtok[0], ps[0][:], ACT.Copy).then_inc(sg_cp[0], 1)
            split_hi(act, Unit(U_CONV + 7))
            for t in range(2):
                act.wait_ge(sg_y, t + 1)
                nc.scalar.activation(yh[:, 6 + t, :], sgy[t], ACT.Copy).then_inc(y_hi, 1)
            act.wait_ge(cv, 10)
            nc.scalar.activation(yh[:, 1, :], kr, ACT.Copy).then_inc(y_hi, 1)

        def act_final(act):
            act_rstd(act, 4, ps[0][:], rstd, 1.0 / D)
            for n in range(KT):
                u = Unit(U_GATE + n)
                if exists(u.plus(2)):
                    split_hi(act, u.plus(2))
                act.wait_ge(evac[u.const % 2], u.half(1))
                nc.scalar.activation(gz[n % 2], gz[n % 2], ACT.Sigmoid).then_inc(gate_s, 1)

        @block.scalar
        def _(act):
            act.preload_act_table_set(LN_EXP)
            for k in range(KT):
                if k % 4 == 0:
                    act.wait_ge(s_x[k // 4], 16)
                nc.scalar.activation(W(11 + k), h[:, k, :], ACT.Square).then_inc(sqs, 1)
            act.wait_ge(s_wab, 16)
            nc.scalar.activation(wh[3][:, 0:P], W(21)[:, 0:P], ACT.Copy).then_inc(g_act, 1)
            split_hi(act, Unit(0))
            act_rstd(act, 1, ps[0][:], W(20), 1.0 / D)
            for k in range(KT):
                if k == 4:
                    split_hi(act, Unit(1))
                act.wait_ge(hn_done, k + 1)
                nc.scalar.activation(xh[:, k, :], W(11 + k), ACT.Copy).then_inc(xh_done, 1)
            act_gdn(act, 0, False, True)
            act_gdn(act, 1, True, True)
            with act.Fori(2, H) as i:
                act_gdn(act, i, True, True)
            act_gdn(act, H, True, False)
            for n in range(KT):
                u = Unit(U_OUT1 + n)
                split_hi(act, u.plus(2))
                act_norm_tile(act, n, u.const % 2, u.half(1), "mlp_g")
            act_mlp(act, U_FF1, 0, True, False, None)
            with act.Fori(1, FF_GROUPS - 1) as g:
                act_mlp(act, U_FF1, g, False, False, None)
            act_mlp(act, U_FF1, FF_GROUPS - 1, False, True, "fn_g")
            act_att(act, 0, False, True)
            act_att(act, 1, True, True)
            with act.Fori(2, PAIRS) as i:
                act_att(act, i, True, True)
            act_att(act, PAIRS, True, True)
            act_conv_sgu(act)
            for n in range(KT):
                u = Unit(U_OUT2 + n)
                split_hi(act, u.plus(2))
                act_norm_tile(act, n, u.const % 2, u.half(1), "n2_g")
            act_mlp(act, U_FF2, 0, True, False, None)
            with act.Fori(1, FF_GROUPS - 1) as g:
                act_mlp(act, U_FF2, g, False, False, None)
            act_mlp(act, U_FF2, FF_GROUPS - 1, False, True, "n3_g")
            act_final(act)

        @block.gpsimd
        def _(pool):
            pool.wait_ge(s_cst, 16)

            def masks(i):
                b = i - 1
                pool.wait_ge(lt_d, i)
                for n in range(1, LEVELS):
                    if n == 1 and (not isinstance(i, int) or i > 1):
                        pool.wait_ge(x_d, b * 6)
                    if n == 2:
                        pool.wait_ge(tt_d, b * LEVELS + 1)
                        pool.wait_ge(l1_d, i)
                    if n > 2:
                        pool.wait_ge(x_d, b * 6 + n - 2)
                    nc.gpsimd.tensor_tensor(c3(Mb[n % 2]), c3(Lt), over_chunks(ch(cst, n)), ALU.mult).then_inc(m_d, 1)
            masks(1)
            with pool.Fori(2, H + 1) as i:
                masks(i)

        def dve_gate_steps(dve):
            ab = small[:, 0:64].rearrange("p (x c h) -> p c x h", x=2, c=C)

            def s1():
                dve.wait_ge(g_pe, 1)
                nc.vector.tensor_copy(W(22)[0:16, :], ps[1][0:16, :]).then_inc(g_dve, 1)

            def s2():
                dve.wait_ge(g_pe, 2)
                src = ps[2][:, 0:64].rearrange("p (c x h) -> p x c h", x=2, c=C)
                dtb = par[:, PC["dt_b"][0]:PC["dt_b"][1]].unsqueeze(1).broadcast_to([P, C, H])
                nc.vector.tensor_tensor(small[:, 0:32].rearrange("p (c h) -> p c h", c=C), src[:, 0], dtb,
                                        ALU.add).then_inc(g_dve, 1)
                nc.vector.tensor_copy(small[:, 32:64].rearrange("p (c h) -> p c h", c=C), src[:, 1]).then_inc(g_dve, 1)
                dve.wait_ge(g_act, 6)
                nc.vector.scalar_tensor_tensor(out=small[:, 64:96], in0=small[:, 0:32], scalar=0.0, in1=small[:, 64:96],
                                               op0=ALU.max, op1=ALU.add).then_inc(g_sp, 1)
                dve.wait_ge(g_sp, 1)
                ea = small[:, 160:168].unsqueeze(1).broadcast_to([P, C, H])
                nc.vector.scalar_tensor_tensor(out=small[:, 96:128].rearrange("p (c h) -> p c h", c=C),
                                               in0=small[:, 64:96].rearrange("p (c h) -> p c h", c=C), scalar=-1.0, in1=ea,
                                               op0=ALU.mult, op1=ALU.mult).then_inc(g_dve, 1)
                nc.vector.tensor_scalar(small[:, 128:160], small[:, 128:160], 1.0, None, ALU.add).then_inc(g_sp, 1)
                dve.wait_ge(g_sp, 2)
                nc.vector.reciprocal(tabs[:, 32:64], small[:, 128:160]).then_inc(g_dve, 1)
                dve.wait_ge(g_pe, 3)
                nc.vector.tensor_copy(tabs[:, 0:32], ps[3][:, 0:32]).then_inc(g_dve, 1)
                nc.vector.tensor_copy(tabs[:, 128:160], ps[3][:, 32:64]).then_inc(g_sp, 1)
                dve.wait_ge(g_sp, 3)
                dve.wait_ge(g_dve, 7)
                nc.vector.tensor_tensor(tabs[:, 96:128], tabs[:, 128:160], tabs[:, 0:32], ALU.subtract).then_inc(g_dve, 1)

            def s3():
                dve.wait_ge(g_act, 8)
                nc.vector.tensor_tensor(tabs[:, 64:96], tabs[:, 64:96], tabs[:, 32:64], ALU.mult).then_inc(g_dve, 1)
                dve.wait_ge(g_pe, 4)
                dve.wait_ge(g_dve, 9)
                nc.vector.tensor_copy(W(23)[0:64, 0:P], ps[4][0:64, 0:P]).then_inc(g_dve, 1)
            return s1, s2, s3

        g_sp = sem("gate_dve_inner")

        def tc(table, c):
            return tcur[:, table * C + c:table * C + c + 1]

        def dve_gdn(dve, i, head, project):
            b = i - 1

            def cur():
                if head:
                    nc.vector.tensor_copy(tcur.unsqueeze(2), tab5[:, :, bass.ds(b, 1)]).then_inc(cur_done, 1)
                if project:
                    nc.vector.tensor_copy(cwc.unsqueeze(2), cwall[:, :, bass.ds(i, 1)]).then_inc(cur_done, 1)

            def conv_steps(n):
                u = Unit(n, i, 4)
                buf = (kc, qc, vc)[n]
                dve.wait_ge(evac[u.const % 2], u.half(1))
                if n == 0:
                    dve.wait_ge(cur_done, i * 2 + 1)
                sec = (1, 0, 2)[n]

                def tap(j):
                    return cwc[:, sec * TAPS + j:sec * TAPS + j + 1]
                nc.vector.tensor_scalar(buf, xpad[:, 3:3 + T], tap(3), None, ALU.mult).then_inc(conv_st, 1)
                yield
                for j in (2, 1, 0):
                    dve.wait_ge(conv_st, i * 12 + 4 * n + 3 - j)
                    nc.vector.scalar_tensor_tensor(out=buf, in0=xpad[:, j:j + T], scalar=tap(j), in1=buf,
                                                   op0=ALU.mult, op1=ALU.add).then_inc(conv_st, 1)
                    yield

            def conv(n):
                for _ in conv_steps(n):
                    pass

            def upd(n):
                dve.wait_ge(xt_d, b * 6 + n) if n == 6 else dve.wait_ge(tx_d, b * 5 + n)
                if n < 6:
                    nc.vector.tensor_tensor(Ti, ps[1][:], Ti, ALU.add).then_inc(t_d, 1)
                    dve.wait_ge(xt_d, b * 6 + n)
                nc.vector.tensor_tensor(TT, ps[2][:], TT, ALU.add).then_inc(tt_d, 1)

            def take(n):
                split_lo(dve, Unit(n + 2, i, 4))
                if n < 3:
                    conv(n)

            cur()
            if head:
                dve.wait_ge(cur_done, i * 2)
                dve.wait_ge(rows_in, i * 32)
                for c in range(C):
                    ins = nc.vector.tensor_scalar(ch(dec, c), ch(grow, c), tc(0, c), 0.0, ALU.subtract, ALU.min)
                ins.then_inc(darg_d, 1)
                dve.wait_ge(dec_d, i)
                nc.vector.tensor_tensor(c3(dec), c3(dec), over_chunks(tri), ALU.mult).then_inc(dm_d, 1)
                dve.wait_ge(dm_d, i)
                nc.vector.tensor_tensor(Lt, dec, brow, ALU.mult).then_inc(lt1_d, 1)
                dve.wait_ge(lt1_d, i)
                dve.wait_ge(kk_d, i)
                nc.vector.tensor_tensor(Lt, ps[0][:], Lt, ALU.mult).then_inc(lt_d, 1)
                dve.wait_ge(lt_d, i)
                nc.vector.tensor_tensor(c3(Mb[0]), c3(Lt), over_chunks(ch(cst, 0)), ALU.mult).then_inc(m0_d, 1)
                dve.wait_ge(qk_d, i)
                nc.vector.tensor_tensor(qkd, ps[1][:], dec, ALU.mult).then_inc(qkd_d, 1)
                dve.wait_ge(m0_d, i)
                nc.vector.tensor_tensor(c3(TT), c3(Mb[0]), over_chunks(ident), ALU.add).then_inc(tt_d, 1)
                split_lo(dve, Unit(1, i, 4))
                dve.wait_ge(l1_d, i)
                nc.vector.tensor_tensor(c3(Ti), c3(ps[4][:]), over_chunks(ident), ALU.add).then_inc(t_d, 1)
                dve.wait_ge(ktr_d, i)
                for c in range(C):
                    nc.vector.tensor_scalar(ch(kb, c), ch(ps[2], c), tc(2, c), None, ALU.mult)
                    ins = nc.vector.tensor_scalar(ch(kd, c), ch(ps[2], c), tc(3, c), None, ALU.mult)
                ins.then_inc(ktok_d, 1)
                if project:
                    split_lo(dve, Unit(2, i, 4))
                upd(1)
                dve.wait_ge(vtr_d, i)
                for c in range(C):
                    ins = nc.vector.tensor_scalar(ch(vb, c), ch(ps[3], c), tc(1, c), None, ALU.mult)
                ins.then_inc(vb_d, 1)
                upd(2)
                if project:
                    conv(0)
                upd(3)
                if not isinstance(i, int) or i > 1:
                    dve_output(dve, b)
                upd(4)
                if project:
                    split_lo(dve, Unit(3, i, 4))
                dve.wait_ge(eg_d, i)
                nc.vector.tensor_tensor(qd, qT, eg, ALU.mult).then_inc(qd_d, 1)
                upd(5)
                if project:
                    conv(1)
                upd(6)
                v_taps = conv_steps(2)
                for c in range(C):
                    dve.wait_ge(v_d, b * 4 + c + 1)
                    nc.vector.tensor_copy(ch(vn, c), ch(ps[3], c)).then_inc(vn_d, 1)
                    if c < C - 1:
                        dve.wait_ge(su_d, b * 3 + c + 1)
                        if c == 0:
                            nc.vector.tensor_copy(S, ps[4][:, 0:P]).then_inc(s_d, 1)
                        else:
                            dve.wait_ge(s_d, b * 3 + c)
                            nc.vector.scalar_tensor_tensor(out=S, in0=S, scalar=tc(4, c), in1=ps[4][:, 0:P],
                                                           op0=ALU.mult, op1=ALU.add).then_inc(s_d, 1)
                    if project and c < 2:
                        next(v_taps)
                        next(v_taps)
                if project:
                    split_lo(dve, Unit(4, i, 4))
            else:
                s1, s2, s3 = dve_gate_steps(dve)
                s1()
                take(0)
                s2()
                take(1)
                s3()
                take(2)
            if project:
                for n, (dst, src, rs) in enumerate(((kT, kc, sk), (qT, qc, sq))):
                    dve.wait_ge(krs, i * 2 + n + 1)
                    sc = (1.0, float(P) ** -0.5)[n]
                    nc.vector.scalar_tensor_tensor(out=dst, in0=src, scalar=sc, in1=rs, op0=ALU.mult, op1=ALU.mult)\
                      .then_inc(kqn, 1)
        def dve_output(dve, i):
            b = i - 1
            if True:
                dve.wait_ge(ors, i)
                nc.vector.tensor_tensor(yb, ps[5][:], osq, ALU.mult).then_inc(o1_d, 1)
                dve.wait_ge(o1_d, i)
                dve.wait_ge(silu_d, i * 4)
                nc.vector.scalar_tensor_tensor(out=yb, in0=yb, scalar=pc("onorm_g"), in1=gs, op0=ALU.mult,
                                               op1=ALU.mult).then_inc(yb_d, 1)
                dve.wait_ge(yb_d, i)
                nc.vector.tensor_scalar(yh[:, bass.ds(b, 1), :], yb.unsqueeze(1), 1.0, None, ALU.mult).then_inc(yh_d, 1)
                dve.wait_ge(yh_d, i)
                nc.vector.tensor_tensor(yl[:, bass.ds(b, 1), :], yb.unsqueeze(1),
                                        yh[:, bass.ds(b, 1), :].bitcast(F32), ALU.subtract).then_inc(yl_d, 1)

        tile_n = [KT]

        def dve_stream_tile(dve, m, u, gname):
            b = u.const % 2
            dve.wait_ge(unit_done, u.number(1))
            nc.vector.tensor_tensor(h[:, m, :], acc[b][:], h[:, m, :], ALU.add).then_inc(evac[b], 1)
            if gname is None:
                return
            n = tile_n[0]
            tile_n[0] += 1
            dve.wait_ge(xh_done, n + 1)
            nc.vector.scalar_tensor_tensor(out=xl[:, m, :], in0=h[:, m, :], scalar=pc(gname, m),
                                           in1=xh[:, m, :].bitcast(F32), op0=ALU.mult, op1=ALU.subtract).then_inc(xl_done, 1)
            dve.wait_ge(sqs, n + 1)
            if m == 0:
                ins = nc.vector.tensor_copy(accb, W(26))
            else:
                dve.wait_ge(accs_t, n)
                ins = nc.vector.tensor_tensor(accb, accb, W(26), ALU.add)
            ins.then_inc(accs_t, 1)
            if gname == "fn_g":
                dve.wait_ge(sqs2, m + 1)
                if m == 0:
                    ins = nc.vector.tensor_copy(sum2, sq2)
                else:
                    dve.wait_ge(sums2, m)
                    ins = nc.vector.tensor_tensor(sum2, sum2, sq2, ALU.add)
                ins.then_inc(sums2, 1)

        def dve_mlp(dve, base, g, first, last, gname):
            for n in range(KT):
                u = Unit(base + n, g, 16)
                b = u.const % 2
                split_lo(dve, u.plus(2))
                cnt = hid_count(base, g) + n
                dve.wait_ge(unit_done, u.number(1))
                if first and n == 0:
                    dve.wait_ge(rst, 2 if base == U_FF1 else 3)
                if not isinstance(cnt, int) or cnt > 0:
                    dve.wait_ge(hid_sq, cnt)
                nc.vector.scalar_tensor_tensor(out=hr, in0=acc[b][:], scalar=0.0, in1=rstd, op0=ALU.max,
                                               op1=ALU.mult).then_inc(evac[b], 1)
                dve.wait_ge(hid_h, cnt + 1)
                nc.vector.tensor_tensor(yl[:, n, :], hs, yh[:, n, :].bitcast(F32), ALU.subtract).then_inc(yl_done, 1)
            for n in range(KT):
                u = Unit(base + KT + n, g, 16)
                if exists(u.plus(2)):
                    split_lo(dve, u.plus(2))
                if last and base == U_FF1 and n == KT - 1:
                    dve.wait_ge(p_hi, 1)
                    nc.vector.tensor_tensor(pl, praw, ph.bitcast(F32), ALU.subtract).then_inc(p_lo, 1)
                dve_stream_tile(dve, n, u, gname if last else None)

        def dve_take(dve, i, n, dst):
            u = Unit(U_ATT + n, i, 4)
            dve.wait_ge(unit_done, u.number(1))
            nc.vector.tensor_tensor(dst, acc[u.const % 2][:], tscale, ALU.mult).then_inc(evac[u.const % 2], 1)

        def dve_att(dve, i, head, project):
            b = i - 1
            past = not isinstance(i, int) or i > 1
            normed = not (isinstance(i, int) and i == PAIRS)

            def lo(n):
                split_lo(dve, Unit(U_ATT + n + 2, i, 4))

            def softplus(n):
                dve.wait_ge(lz_d, b * 2 + n + 1)
                if n > 0 or past:
                    dve.wait_ge(lw_d, b * 2 + n)
                for z, (at, w) in enumerate(ZBANK):
                    last = nc.vector.scalar_tensor_tensor(out=spz[:, at:at + w], in0=ps[z][:, 0:w], scalar=0.0,
                                                          in1=az[:, at:at + w], op0=ALU.max, op1=ALU.add)
                last.then_inc(sp_d, 1)

            def normal(n):
                dve.wait_ge(qk_rs, i * 2 + n + 1)
                if head:
                    dve.wait_ge(z_d, i * 2)
                nc.vector.scalar_tensor_tensor(out=(qn, kn)[n], in0=(qr, kr)[n], scalar=pc(("q_g8", "k_g")[n]),
                                               in1=(qs, ks)[n], op0=ALU.mult, op1=ALU.mult).then_inc(qk_n, 1)

            def gating():
                u = Unit(U_ATT + 3, i, 4)
                dve.wait_ge(unit_done, u.number(1))
                if isinstance(i, int):
                    nc.vector.tensor_tensor(ch5(uv, i), acc[u.const % 2][:], tscale, ALU.mult).then_inc(evac[u.const % 2], 1)
                else:
                    dst = uv.rearrange("p (j t) -> p j t", t=T)[:, bass.ds(i, 1), :]
                    nc.vector.tensor_tensor(dst, acc[u.const % 2][:].unsqueeze(1), tscale.unsqueeze(1), ALU.mult)\
                      .then_inc(evac[u.const % 2], 1)

            if not head:
                split_lo(dve, Unit(U_PLE + 2))
                split_lo(dve, Unit(U_PLE + 3))
                lo(0)
                dve.wait_ge(rs2, 1)
                dve.wait_ge(rs2_mm, 2)
                nc.vector.tensor_tensor(r1, ps[1][:], rf, ALU.mult).then_inc(scale_d, 1)
                dve.wait_ge(scale_d, 1)
                nc.vector.tensor_tensor(r1, r1, rf, ALU.mult).then_inc(scale_d, 1)
                dve.wait_ge(rs2, 2)
                nc.vector.tensor_tensor(tscale, r1, rf, ALU.mult).then_inc(scale_d, 1)
                dve.wait_ge(scale_d, 3)
                dve_take(dve, i, 0, qr)
                lo(1)
                dve_take(dve, i, 1, kr)
                lo(2)
                dve_take(dve, i, 2, vr)
                lo(3)
                normal(0)
                normal(1)
                dve.wait_ge(pp_out[0], 16)
                gating()
                for m in range(KT):
                    nc.vector.scalar_tensor_tensor(out=h[:, m, :], in0=h[:, m, :], scalar=pc("fin_g", m), in1=rf,
                                                   op0=ALU.mult, op1=ALU.mult).then_inc(h_scaled, 1)
                return
            lo(0)
            softplus(0)
            dve_take(dve, i, 0, qr if normed else conv_in[0])
            lo(1)
            dve_take(dve, i, 1, kr if normed else conv_in[1])
            softplus(1)
            lo(2)
            if normed:
                normal(0)
                dve.wait_ge(vt_mm, i)
            dve_take(dve, i, 2, vr if normed else conv_in[2])
            if not normed:
                dve_conv(dve, 0)
            lo(3)
            if normed:
                normal(1)
                gating()
            else:
                dve_take(dve, i, 3, conv_in[3])
            dve.wait_ge(av_d, i * 2)
            nc.vector.tensor_scalar(yh[:, bass.ds(b + 2, 1), :], ps[3][:].unsqueeze(1), 1.0, None, ALU.mult)\
              .then_inc(ah_d, 1)
            dve.wait_ge(ah_d, i)
            nc.vector.tensor_tensor(yl[:, bass.ds(b + 2, 1), :], ps[3][:].unsqueeze(1),
                                    yh[:, bass.ds(b + 2, 1), :].bitcast(F32), ALU.subtract).then_inc(al_d, 1)

        def dve_conv(dve, t):
            ci, hi_, bi = conv_in[3 * t:3 * t + 3]
            dst = (qr, kr)[t]
            last = U_CONV + 3 * t + 2
            for u in (last - 1, last):
                dve.wait_ge(evac[u % 2], u // 2 + 1)
            nc.vector.tensor_tensor(xpad[:, 3:3 + T], ci, hi_, ALU.mult).then_inc(cv, 1)
            dve.wait_ge(cv, 5 * t + 1)
            nc.vector.tensor_scalar(dst, xpad[:, 3:3 + T], pc("conv2_w", 3 * t + 2), None, ALU.mult).then_inc(cv, 1)
            for n, j in enumerate((1, 0)):
                dve.wait_ge(cv, 5 * t + 2 + n)
                nc.vector.scalar_tensor_tensor(out=dst, in0=xpad[:, 1 + j:1 + j + T], scalar=pc("conv2_w", 3 * t + j),
                                               in1=dst, op0=ALU.mult, op1=ALU.add).then_inc(cv, 1)
            dve.wait_ge(cv, 5 * t + 4)
            nc.vector.tensor_tensor(dst, dst, bi, ALU.mult).then_inc(cv, 1)

        def dve_conv_sgu(dve):
            def y_low(n, k, src):
                dve.wait_ge(y_hi, n + 1)
                nc.vector.tensor_tensor(yl[:, k, :], src, yh[:, k, :].bitcast(F32), ALU.subtract).then_inc(y_lo, 1)

            def gate(t):
                dve.wait_ge(sg_mm, t + 1)
                bias = bsT[:, t * P:(t + 1) * P].unsqueeze(1).broadcast_to([P, C, P])
                nc.vector.tensor_tensor(c3(sgy[t]), c3(ps[2 + t][:]), bias, ALU.add).then_inc(sg_b, 1)
                dve.wait_ge(sg_b, t + 1)
                nc.vector.tensor_tensor(sgy[t], sgy[t], ch5(uv, t), ALU.mult).then_inc(sg_y, 1)

            dve.wait_ge(s_cst, 32)
            nc.vector.tensor_tensor(c3(wsT), c3(wsT), over_chunks(tri), ALU.mult).then_inc(sg_w, 1)
            split_lo(dve, Unit(U_CONV + 6))
            for t in range(2):
                dve.wait_ge(sg_rs, t + 1)
                nc.vector.scalar_tensor_tensor(out=(qn, kn)[t], in0=ch5(uv, 2 + t), scalar=pc("sgu_g", t),
                                               in1=(qs, ks)[t], op0=ALU.mult, op1=ALU.mult).then_inc(sg_n, 1)
            dve_take(dve, PAIRS, 4, conv_in[4])
            y_low(0, 0, qr)
            dve.wait_ge(sg_tr, 2)
            nc.vector.tensor_copy(vtok[1], ps[1][:]).then_inc(sg_cp[1], 1)
            split_lo(dve, Unit(U_CONV + 7))
            gate(0)
            gate(1)
            y_low(1, 6, sgy[0])
            y_low(2, 7, sgy[1])
            dve_take(dve, PAIRS, 5, conv_in[5])
            dve_conv(dve, 1)
            y_low(3, 1, kr)

        def dve_final(dve):
            def finish(n):
                dve.wait_ge(gate_s, n + 1)
                nc.vector.tensor_tensor(gz[n % 2], gz[n % 2], ch5(pp, n), ALU.mult).then_inc(gate_p, 1)
                dve.wait_ge(gate_p, n + 1)
                nc.vector.tensor_tensor(h[:, n, :], h[:, n, :], gz[n % 2], ALU.add).then_inc(h_final, 1)

            dve.wait_ge(rst, 4)
            dve.wait_ge(pp_in, 32)
            for n in range(KT):
                u = Unit(U_GATE + n)
                if exists(u.plus(2)):
                    split_lo(dve, u.plus(2))
                dve.wait_ge(unit_done, u.number(1))
                if n >= 2:
                    dve.wait_ge(h_final, n - 1)
                nc.vector.tensor_tensor(gz[n % 2], acc[u.const % 2][:], rstd, ALU.mult).then_inc(evac[u.const % 2], 1)
                if n > 0:
                    finish(n - 1)
            finish(KT - 1)

        @block.vector
        def _(dve):
            nc.vector.memset(xpad[:, 0:3], 0.0).then_inc(zp, 1)
            for k in range(KT):
                dve.wait_ge(sqs, k + 1)
                if k == 0:
                    nc.vector.tensor_copy(accb, W(11)).then_inc(accs_t, 1)
                else:
                    dve.wait_ge(accs_t, k)
                    nc.vector.tensor_tensor(accb, accb, W(11 + k), ALU.add).then_inc(accs_t, 1)
            dve.wait_ge(g_act, 1)
            nc.vector.tensor_tensor(wl[3][:, 0:P], W(21)[:, 0:P], wh[3][:, 0:P].bitcast(F32), ALU.subtract).then_inc(g_dve, 1)
            split_lo(dve, Unit(0))
            dve.wait_ge(s_par, 32)
            nc.vector.tensor_tensor(par[:, NPAR:NPAR + KT], par[:, PC["fin_g"][0]:PC["fin_g"][1]],
                                    par[:, PC["n1_g"][0]:PC["n1_g"][1]], ALU.mult)
            nc.vector.tensor_scalar(par[:, NPAR + KT:NPAR + KT + 1], pc("q_g"), HD ** -0.5, None, ALU.mult)
            dve.wait_ge(rst, 1)
            for k in range(KT):
                nc.vector.scalar_tensor_tensor(out=W(11 + k), in0=h[:, k, :], scalar=pc("mix_g", k), in1=W(20),
                                               op0=ALU.mult, op1=ALU.mult).then_inc(hn_done, 1)
                if k > 0:
                    dve.wait_ge(xh_done, k)
                    nc.vector.tensor_tensor(xl[:, k - 1, :], W(10 + k), xh[:, k - 1, :].bitcast(F32),
                                            ALU.subtract).then_inc(xl_done, 1)
            dve.wait_ge(xh_done, KT)
            nc.vector.tensor_tensor(xl[:, KT - 1, :], W(10 + KT), xh[:, KT - 1, :].bitcast(F32),
                                    ALU.subtract).then_inc(xl_done, 1)
            split_lo(dve, Unit(1))
            dve_gdn(dve, 0, False, True)
            dve_gdn(dve, 1, True, True)
            with dve.Fori(2, H) as i:
                dve_gdn(dve, i, True, True)
            dve_gdn(dve, H, True, False)
            dve_output(dve, H)
            for n in range(KT):
                u = Unit(U_OUT1 + n)
                split_lo(dve, u.plus(2))
                dve_stream_tile(dve, n, u, "mlp_g")
            dve_mlp(dve, U_FF1, 0, True, False, None)
            with dve.Fori(1, FF_GROUPS - 1) as g:
                dve_mlp(dve, U_FF1, g, False, False, None)
            dve_mlp(dve, U_FF1, FF_GROUPS - 1, False, True, "fn_g")
            dve_att(dve, 0, False, True)
            dve_att(dve, 1, True, True)
            with dve.Fori(2, PAIRS) as i:
                dve_att(dve, i, True, True)
            dve_att(dve, PAIRS, True, True)
            dve_conv_sgu(dve)
            for n in range(KT):
                u = Unit(U_OUT2 + n)
                split_lo(dve, u.plus(2))
                dve_stream_tile(dve, n, u, "n2_g")
            dve_mlp(dve, U_FF2, 0, True, False, None)
            with dve.Fori(1, FF_GROUPS - 1) as g:
                dve_mlp(dve, U_FF2, g, False, False, None)
            dve_mlp(dve, U_FF2, FF_GROUPS - 1, False, True, "n3_g")
            dve_final(dve)



def constants():
    j, i = np.mgrid[0:P, 0:P]
    keep = np.concatenate([j == i, j >= 0, j <= i], axis=1).astype(np.float32)
    levels = []
    for n in range(LEVELS):
        s = 1 << n
        levels.append((j // (2 * s) == i // (2 * s)) & (j // s % 2 == 0) & (i // s % 2 == 1))
    levels = np.where(np.concatenate(levels, axis=1), np.float32(-1), np.float32(0))
    second = np.concatenate([np.where(j >= i, -1.0, 0.0), np.full((P, P), -1.0), np.where(i <= j, NEG, 0.0),
                             np.where(j // HD == i // HD, 1.0, 0.0)], axis=1).astype(np.float32)
    return keep, levels, second


def pack(weights):
    def unit(w, col, row=0):
        return w[row:row + D, col:col + P].reshape(KT, P, P).transpose(1, 0, 2).reshape(P, D)

    w_in, w_out, w1, w2, w_in2, w_out2, w12, w22, proj, gate = weights
    units = [unit(w_in, sec * D + i * P) for i in range(H) for sec in (1, 0, 2, 3)]
    units += [unit(w_out, m * P) for m in range(KT)]
    mlp = [[unit(a, g * D + n * P) for n in range(KT)] + [unit(b, n * P, g * D) for n in range(KT)]
           for a, b in ((w1, w2), (w12, w22)) for g in range(FF_GROUPS)]
    units += sum(mlp[:FF_GROUPS], [])
    units += [proj[:, n * T:(n + 1) * T].reshape(2, P, T).transpose(1, 0, 2).reshape(P, D) for n in range(2)]
    heads = 2 * HD * PAIRS
    conv = 2 * P
    for j in range(PAIRS):
        units += [unit(w_in2, 3 * conv + sec * heads + j * P) for sec in range(4)]
    units += [unit(w_in2, sec * conv + t * P) for t in range(2) for sec in (1, 2, 0)]
    units += [unit(w_out2, m * P) for m in range(KT)]
    units += sum(mlp[FF_GROUPS:], [])
    units += [unit(gate, m * P) for m in range(KT)]
    assert len(units) == U_END
    return np.stack(units, axis=1)


def kernel(**x):
    import concourse.bacc as bacc
    from concourse.bass_utils import run_bass_kernel_spmd

    return launch(x, bacc, run_bass_kernel_spmd)


def launch(x, bacc, run):
    def tiles(v):
        return np.asarray(v).reshape(-1, P).T

    x = {k: np.asarray(v) for k, v in x.items()}
    cw = x["gdn_conv_w"][0].reshape(TAPS, 3, H, P).transpose(3, 1, 0, 2).reshape(P, -1)
    cw2 = x["conv_w_2"][0].reshape(TAPS2, 2, P).transpose(2, 1, 0).reshape(P, -1)
    params = np.concatenate([
        tiles(x["norm_mix_g"][0]), tiles(x["norm_mlp_g"][0]), tiles(x["final_norm_g"]), tiles(x["norm1_g_2"][0]),
        tiles(x["norm2_g_2"][0]), tiles(x["norm3_g_2"][0]), cw, cw2, tiles(x["gdn_o_norm_g"][0]),
        tiles(np.tile(x["q_norm_g_2"][0], 2)), tiles(np.tile(x["k_norm_g_2"][0], 2)), tiles(x["sgu_norm_g_2"][0]),
        np.broadcast_to(x["gdn_a_log"][0], (P, H)), np.broadcast_to(x["gdn_dt_bias"][0], (P, H)),
    ], axis=1)
    keep, levels, second = constants()
    sgu_w = x["sgu_w_2"][0].transpose(2, 0, 1).reshape(P, -1)
    sgu_b = np.repeat(x["sgu_b_2"][0].reshape(2, 2, P), HD, axis=1).transpose(1, 0, 2).reshape(P, -1)
    arrays = {
        "xT": x["x"][0].T, "pT": x["p_2"][0, 0].T, "params": params, "keep": keep, "levels": levels,
        "cst2": np.concatenate([second, sgu_w, sgu_b], axis=1),
        "w_ab": x["gdn_w_in"][0][:, 4 * D:].reshape(KT, P, 2 * H).transpose(1, 0, 2).reshape(P, -1),
        "weights": pack([x[k][0] for k in ("gdn_w_in", "gdn_w_out", "mlp_w1", "mlp_w2", "w_in_2", "w_out_2",
                                           "w_ff1_2", "w_ff2_2", "w_ple_proj_2", "w_ple_gate_2")]),
    }
    arrays = {k: np.ascontiguousarray(v) for k, v in arrays.items()}
    nc = bacc.Bacc("TRN2", target_bir_lowering=False, num_devices=1)
    a = {k: nc.dram_tensor("in_" + k, v.shape, mybir.dt.from_np(v.dtype), kind="ExternalInput").ap() for k, v in arrays.items()}
    out = nc.dram_tensor("outT", (D, T), F32, kind="ExternalOutput").ap()
    build(nc, a, out)
    r = run(nc, [{"in_" + k: v for k, v in arrays.items()}], core_ids=[0])
    return np.ascontiguousarray(r.results[0]["outT"].T)[None]
```

```python
from contextlib import ExitStack

import numpy as np

import concourse.bass as bass
from concourse import mybir

ACT = mybir.ActivationFunctionType
ALU = mybir.AluOpType
F32 = mybir.dt.float32
F32R = mybir.dt.float32r

P = 128
T = 512
D = 1024
KT = D // P
H = 8
C = T // P
EPS = 1e-6
LEVELS = 7
FF_GROUPS = 4
PAIRS = 4
TAPS = 4
HD = 64
TAPS2 = 3
LN_EXP = "natural_log_exp_and_others"
NEG = -1e30

U_OUT1 = 4 * H
U_FF1 = U_OUT1 + KT
U_PLE = U_FF1 + 16 * FF_GROUPS
U_ATT = U_PLE + 2
U_CONV = U_ATT + 4 * PAIRS
U_OUT2 = U_CONV + 6
U_FF2 = U_OUT2 + KT
U_GATE = U_FF2 + 16 * FF_GROUPS
U_END = U_GATE + KT

PC = {}
_n = 0
for _name, _width in (("mix_g", 8), ("mlp_g", 8), ("fin_g", 8), ("n1_g", 8), ("n2_g", 8), ("n3_g", 8),
                      ("conv_w", 96), ("conv2_w", 6), ("onorm_g", 1), ("q_g", 1), ("k_g", 1),
                      ("sgu_g", 2), ("a_log", 8), ("dt_b", 8)):
    PC[_name] = (_n, _n + _width)
    _n += _width
NPAR = _n

ZAT = ((0, 0, 0), (1, 0, T), (2, 0, 2 * T), (1, 3 * P, T + 3 * P))
ZBANK = ((0, T), (T, T), (2 * T, 2 * P))
ZW = 2 * T + 2 * P

CST = 1280


class Unit:

    def __init__(self, const, reg=0, per=0):
        if isinstance(reg, int):
            const, reg, per = const + reg * per, 0, 0
        assert per % 4 == 0
        self.const, self.reg, self.per = const, reg, per

    def plus(self, n):
        return Unit(self.const + n, self.reg, self.per)

    def number(self, n=0):
        return self.const + n if self.per == 0 else self.reg * self.per + (self.const + n)

    def half(self, n=0):
        return self.const // 2 + n if self.per == 0 else self.reg * (self.per // 2) + (self.const // 2 + n)

    def known_below(self, n):
        return self.per == 0 and self.const < n


def build(nc, a, out):
    ctx = ExitStack()
    with ctx:
        def sb(name, shape, dt=F32):
            return ctx.enter_context(nc.sbuf_tensor(name, shape, dt))

        def bank(name):
            return ctx.enter_context(nc.psum_tensor(name, [P, T], F32))

        def sem(name):
            return ctx.enter_context(nc.semaphore(name))

        h = sb("h", [P, KT, T])
        xh, xl = sb("xh", [P, KT, T], F32R), sb("xl", [P, KT, T], F32R)
        yh, yl = sb("yh", [P, KT, T], F32R), sb("yl", [P, KT, T], F32R)
        raw = [sb(f"raw{n}", [P, D]) for n in range(2)]
        wh = [sb(f"wh{n}", [P, D], F32R) for n in range(4)]
        wl = [sb(f"wl{n}", [P, D], F32R) for n in range(4)]
        cst = sb("cst", [P, CST])
        keep = sb("kept", [P, 3 * P])
        par = sb("par", [P, NPAR + KT + 1])
        xpad = sb("xpad", [P, T + 4])
        work = sb("work", [P, 29 * T])
        ident, ones, tri = keep[:, 0:P], keep[:, P:2 * P], keep[:, 2 * P:3 * P]

        def W(n, m=1):
            return work[:, n * T:(n + m) * T]

        def ch(ap, c):
            return ap[:, c * P:(c + 1) * P]

        def c3(ap):
            return ap.rearrange("p (c t) -> p c t", c=C)

        def ch5(ap, n):
            return ap[:, n * T:(n + 1) * T]

        def over_chunks(m):
            return m.unsqueeze(1).broadcast_to([P, C, P])

        def halves(ap, n, second):
            return ap.rearrange("p (g two s) -> p g two s", two=2, s=1 << n)[:, :, second, :]

        def pc(name, n=0):
            lo = {"fn_g": NPAR, "q_g8": NPAR + KT}.get(name) or PC[name][0]
            return par[:, lo + n:lo + n + 1]

        kc, qc, vc, sk, sq = W(0), W(1), W(2), W(3), W(4)
        kT, qT, graw, gs, grow, brow = W(5), W(6), W(7), W(8), W(9), W(10)
        dec, Lt, qkd, Mb = W(11), W(12), W(13), [W(14), W(15)]
        Ti, TT, Xs, kb, kd, vb = W(16), W(17), W(18), W(19), W(20), W(21)
        nw, qd, vn, eg, osq, yb = W(22), W(23), W(24), W(25), W(26), W(27)
        S = W(28)[:, 0:P]
        tabs = W(28)[:, 128:288]
        tab5 = tabs.rearrange("p (x h) -> p x h", h=H)
        tcur = W(28)[:, 288:308]
        cwc = W(28)[:, 308:320]
        small = W(28)[:, 320:512]
        cwall = par[:, PC["conv_w"][0]:PC["conv_w"][1]].rearrange("p (x h) -> p x h", h=H)

        acc = [bank(f"acc{n}") for n in range(2)]
        ps = [bank(f"ps{n}") for n in range(6)]

        proj = nc.dram_tensor("proj", (P, KT, T), F32, kind="Internal").ap()
        rows = nc.dram_tensor("rows", (2, C, H, P), F32, kind="Internal").ap()

        s_par, s_x, s_cst, s_wab = sem("params_in"), [sem(f"x_in{n}") for n in range(4)], sem("const_in"), sem("wab_in")
        w_in = [sem(f"weights_in{n}") for n in range(2)]
        hi_done, lo_done, unit_done = sem("hi_done"), sem("lo_done"), sem("unit_done")
        evac = [sem(f"acc_evacuated{n}") for n in range(2)]
        sqs, accs_t, rs_mm, lnd, rst = sem("squares"), sem("sq_sums"), sem("rstd_mm"), sem("ln_done"), sem("rstd_ready")
        xh_done, xl_done = sem("xh_done"), sem("xl_done")
        g_act, g_dve, g_pe, g_dma = sem("gate_act"), sem("gate_dve"), sem("gate_pe"), sem("gate_rows_out")
        rows_in, cur_done, conv_st = sem("rows_in"), sem("cur_done"), sem("conv_steps")
        silu_d, ksq_d, kss_mm, kln, krs, kqn = (sem("silu_done"), sem("kq_squared"), sem("kq_sums"), sem("kq_ln"),
                                               sem("kq_rstd"), sem("kq_normed"))
        kk_d, qk_d, ktr_d, vtr_d = sem("kk_done"), sem("qk_done"), sem("k_transposed"), sem("v_transposed")
        darg_d, dec_d, dm_d, eg_d = sem("decay_arg"), sem("decay_exp"), sem("decay_masked"), sem("eg_done")
        lt1_d, lt_d, qkd_d, ktok_d, vb_d, qd_d = (sem("lt_half"), sem("lt_done"), sem("qkd_done"), sem("kbkd_done"),
                                                  sem("vb_done"), sem("qd_done"))
        m_d, l1_d, t_d, tt_d, x_d, xs_d, tx_d, xt_d = (sem("m_done"), sem("m1_transposed"), sem("t_updated"),
                                                       sem("tt_updated"), sem("x_done"), sem("x_copied"),
                                                       sem("tx_done"), sem("xt_done"))
        w_d, nw_d, v_d, vn_d, su_d, s_d, o_d = (sem("w_done"), sem("nw_done"), sem("v_done"), sem("vn_done"),
                                                sem("state_mm"), sem("s_done"), sem("o_done"))
        osq_d, oss_d, oln, ors, o1_d, yb_d, yh_d, yl_d = (sem("o_squared"), sem("o_sums"), sem("o_ln"), sem("o_rstd"),
                                                   sem("o_scaled"), sem("y_done"), sem("yh_done"), sem("yl_done"))
        out_d = sem("out_stored")
        zp = sem("zero_pad")
        m0_d, tc_d = sem("m0_done"), sem("tt_copied")
        x_sq = sem("x_square_sums")
        s_keep, x_hi, x_lo, xr_d = sem("kept_in"), sem("x_hi"), sem("x_lo"), sem("x_scaled")
        y_free = sem("yh_read")
        sqs2, sums2, rs2_mm, ln2, rs2 = (sem("squares2"), sem("sq_sums2"), sem("rstd2_mm"), sem("ln2_done"),
                                         sem("rstd2_ready"))
        scale_d, h_scaled = sem("token_scale"), sem("stream_scaled")
        vt_mm, vt_d, z_d, abs_d, ez_d, lz_d, sp_d = (sem("v2_transposed"), sem("v2_copied"), sem("scores_ready"),
                                                    sem("abs_scores"), sem("exp_scores"), sem("ln_scores"),
                                                    sem("softplus_done"))
        lw_d, aw_d, av_d, ah_d, al_d = (sem("log_weights"), sem("weights_ready"), sem("attended"),
                                        sem("attended_hi"), sem("attended_lo"))
        qk_sq, qk_sum, qk_ln, qk_rs, qk_n = (sem("qk2_squared"), sem("qk2_sums"), sem("qk2_ln"), sem("qk2_rstd"),
                                             sem("qk2_normed"))
        cv, y_hi, y_lo = sem("conv2_steps"), sem("y2_hi"), sem("y2_lo")
        gelu_d, sg_sq, sg_sum, sg_ln, sg_rs, sg_n, sg_tr, sg_w, sg_mm, sg_b, sg_y = (
            sem("gelu_done"), sem("sgu_squared"), sem("sgu_sums"), sem("sgu_ln"), sem("sgu_rstd"), sem("sgu_normed"),
            sem("sgu_transposed"), sem("sgu_masked"), sem("sgu_mm"), sem("sgu_biased"), sem("sgu_y"))
        p_in, p_hi, p_lo, ple_mm, ple_cp = sem("p_in"), sem("p_hi"), sem("p_lo"), sem("ple_tiles"), sem("ple_copied")
        pp_out, pp_in = [sem("proj_out0"), sem("proj_out1")], sem("proj_in")
        gate_s, gate_p, h_final = sem("gate_sigmoid"), sem("gated"), sem("h_final")

        qr, kr, qs, ks = W(0), W(1), W(2), W(3)
        qn, kn, vr, vt = W(4), W(5), W(6), W(7)
        uv = W(8, 4)
        az, spz, aw = W(12, 3)[:, 0:ZW], W(15, 3)[:, 0:ZW], W(18, 3)[:, 0:ZW]
        tscale = W(22)
        conv_in = [W(23 + n) for n in range(6)]
        sq2, sum2, rf, r1 = W(20), W(19), W(18), W(17)
        ph, pl = yh[:, 0:2, :], yl[:, 0:2, :]
        praw = W(12, 2).rearrange("p (k t) -> p k t", k=2)
        stage = [W(8, 4), W(12, 4)]
        pp = W(4, 8)
        pp3 = pp.rearrange("p (k t) -> p k t", t=T)
        gz = [W(14), W(15)]
        vtok, sgy = [W(12), W(13)], [W(14), W(15)]
        sg_cp = [sem("sgu_v_copied0"), sem("sgu_v_copied1")]
        sph, spl = [yh[:, k, :] for k in (0, 1, 6)], [yl[:, k, :] for k in (0, 1, 6)]
        ntri_r, nones_r, negm_r, ident_r = (ch(yh[:, 7, :], n) for n in range(4))
        sh_d, sl_d, tri_d = sem("softplus_hi"), sem("softplus_lo"), sem("triangle_copied")
        blk = ch(cst, 3)
        wsT, bsT = cst[:, 4 * P:8 * P], cst[:, 8 * P:10 * P]

        block = ctx.enter_context(nc.Block())

        def exists(u):
            return u.per != 0 or u.const < U_END

        def load_unit(sp, n, b):
            if not isinstance(n, int) or n >= 2:
                sp.wait_ge(lo_done, n - 1)
            sp.dma_start(raw[b][:].unsqueeze(1), a["weights"][:, bass.ds(n, 1), :]).then_inc(w_in[b], 16)

        def load_units(sp, first, last):
            with sp.Fori(first // 2, last // 2) as n:
                for b in range(2):
                    load_unit(sp, n * 2 + b, b)

        def split_hi(act, u):
            act.wait_ge(w_in[u.const % 2], u.half(1) * 16)
            if not u.known_below(4):
                act.wait_ge(unit_done, u.number(-3))
            nc.scalar.activation(wh[u.const % 4][:], raw[u.const % 2][:], ACT.Copy).then_inc(hi_done, 1)

        def split_lo(dve, u):
            dve.wait_ge(hi_done, u.number(1))
            if not u.known_below(4):
                dve.wait_ge(unit_done, u.number(-3))
            nc.vector.tensor_tensor(wl[u.const % 4][:], raw[u.const % 2][:], wh[u.const % 4][:].bitcast(F32),
                                    ALU.subtract).then_inc(lo_done, 1)

        def accumulator(u):
            if u.per == 0 and u.const in (U_OUT1 + 2, U_OUT1 + 3):
                return ps[(u.const - U_OUT1 - 2) * 2]
            return acc[u.const % 2]

        def unit_steps(pe, u, mh, ml, gate=None, order=range(KT), freed=None):
            b, s, dst = u.const % 2, u.const % 4, accumulator(u)
            pe.wait_ge(lo_done, u.number(1))
            if not u.known_below(2) and dst is acc[b]:
                beside = u.per == 0 and u.const in (U_OUT1 + 4, U_OUT1 + 5)
                pe.wait_ge(evac[b], u.half(-1 if beside else 0))
            for n, k in enumerate(order):
                if gate is not None:
                    gate(k)
                hi, lo = ch(wh[s], k), ch(wl[s], k)
                nc.tensor.matmul(dst[:], hi, mh[:, k, :], start=(n == 0), stop=False)
                nc.tensor.matmul(dst[:], hi, ml[:, k, :], start=False, stop=False)
                mm = nc.tensor.matmul(dst[:], lo, mh[:, k, :], start=False, stop=(n == KT - 1))
                if n == KT - 1:
                    mm.then_inc(unit_done, 1)
                elif n == 1 and freed is not None:
                    mm.then_inc(freed, 1)
                yield

        def run_unit(pe, u, mh, ml, gate=None, order=range(KT), freed=None):
            for _ in unit_steps(pe, u, mh, ml, gate, order, freed):
                pass

        @block.sync
        def _(sp):
            sp.dma_start(par[:, 0:NPAR], a["params"]).then_inc(s_par, 16)
            load_unit(sp, 0, 0)
            for n in range(4):
                sp.dma_start(h[:, 2 * n:2 * n + 2, :],
                             a["xT"].rearrange("(k p) t -> p k t", p=P)[:, 2 * n:2 * n + 2, :]).then_inc(s_x[n], 16)
                if n == 1:
                    sp.dma_start(keep[:], a["keep"]).then_inc(s_keep, 16)
            sp.dma_start(W(21)[:, 0:P], a["w_ab"]).then_inc(s_wab, 16)
            load_unit(sp, 1, 1)
            sp.dma_start(cst[:, 0:LEVELS * P], a["levels"]).then_inc(s_cst, 16)
            load_units(sp, 2, U_OUT1 + 4)
            sp.wait_ge(m0_d, H)
            sp.wait_ge(m_d, H * (LEVELS - 1))
            sp.dma_start(cst[:], a["cst2"]).then_inc(s_cst, 16)
            load_units(sp, U_OUT1 + 4, U_FF1)
            sp.wait_ge(o_d, H)
            sp.dma_start(praw, a["pT"].rearrange("(k p) t -> p k t", p=P)).then_inc(p_in, 16)
            load_units(sp, U_FF1, U_FF2)
            sp.wait_ge(y_lo, 4)
            for n in range(2):
                sp.wait_ge(pp_out[n], 16)
                sp.dma_start(pp3[:, 4 * n:4 * n + 4, :], proj[:, 4 * n:4 * n + 4, :]).then_inc(pp_in, 16)
            load_units(sp, U_FF2, U_END)
            for m in range(KT):
                sp.wait_ge(h_final, m + 1)
                sp.dma_start(out[m * P:(m + 1) * P, :], h[:, m, :]).then_inc(out_d, 16)
            sp.wait_ge(out_d, 16 * KT)

        def pe_gate_steps(pe):
            def mm():
                pe.wait_ge(g_dve, 1)
                for k in range(KT):
                    hi, lo = wh[3][:, k * 16:(k + 1) * 16], wl[3][:, k * 16:(k + 1) * 16]
                    nc.tensor.matmul(ps[1][0:16, :], hi, yh[:, k, :], start=(k == 0), stop=False)
                    nc.tensor.matmul(ps[1][0:16, :], hi, yl[:, k, :], start=False, stop=False)
                    last = nc.tensor.matmul(ps[1][0:16, :], lo, yh[:, k, :], start=False, stop=(k == KT - 1))
                last.then_inc(g_pe, 1)

            def tr():
                pe.wait_ge(g_dve, 2)
                for c in range(C):
                    last = nc.tensor.transpose(ps[2][:, c * 16:(c + 1) * 16], ch(W(22), c)[0:16, :], ident[0:16, 0:16])
                last.then_inc(g_pe, 1)

            def cum():
                pe.wait_ge(g_dve, 5)
                nc.tensor.matmul(ps[3][:, 0:32], tri, small[:, 96:128], start=True, stop=True)
                nc.tensor.matmul(ps[3][:, 32:64], ones, small[:, 96:128], start=True, stop=True).then_inc(g_pe, 1)

            def row():
                pe.wait_ge(g_dve, 8)
                nc.tensor.transpose(ps[4][0:64, 0:P], tabs[:, 0:64], ident).then_inc(g_pe, 1)

            return [mm, tr, cum, row]

        def pe_head_steps(pe, i):
            b = i - 1

            def first():
                pe.wait_ge(kqn, i * 2 - 1)
                for c in range(C):
                    last = nc.tensor.matmul(ch(ps[0], c), ch(kT, c), ch(kT, c), start=True, stop=True)
                last.then_inc(kk_d, 1)
                pe.wait_ge(kqn, i * 2)
                for c in range(C):
                    last = nc.tensor.matmul(ch(ps[1], c), ch(kT, c), ch(qT, c), start=True, stop=True)
                last.then_inc(qk_d, 1)
                for c in range(C):
                    last = nc.tensor.transpose(ch(ps[2], c), ch(kT, c), ident)
                last.then_inc(ktr_d, 1)
                pe.wait_ge(silu_d, i * 4 - 1)
                for c in range(C):
                    last = nc.tensor.transpose(ch(ps[3], c), ch(vc, c), ident)
                last.then_inc(vtr_d, 1)

            def level1():
                pe.wait_ge(m0_d, i)
                if not isinstance(i, int) or i > 1:
                    pe.wait_ge(oln, b)
                for c in range(C):
                    last = nc.tensor.transpose(ch(ps[4], c), ch(Mb[0], c), ident)
                last.then_inc(l1_d, 1)

            def x(n):
                def step():
                    pe.wait_ge(m_d, b * 6 + n)
                    pe.wait_ge(t_d, b * 6 + n)
                    for c in range(C):
                        last = nc.tensor.matmul(ch(ps[0], c), ch(Mb[n % 2], c), ch(Ti, c), start=True, stop=True)
                    last.then_inc(x_d, 1)
                    if n > 1:
                        for c in range(C):
                            last = nc.tensor.transpose(ch(ps[2], c), ch(Ti, c), ident)
                        last.then_inc(xt_d, 1)
                return step

            def tx(n):
                def step():
                    pe.wait_ge(xs_d, b * 6 + n)
                    if n == 1:
                        pe.wait_ge(tt_d, b * 2 + 1)
                    else:
                        pe.wait_ge(tc_d, b * 5 + n - 1)
                    if n == 1:
                        pe.wait_ge(qkd_d, i)
                        pe.wait_ge(ktok_d, i)
                    if n < 6:
                        for c in range(C):
                            last = nc.tensor.matmul(halves(ch(ps[1], c), n, 0), ch(TT, c), halves(ch(Xs, c), n, 0),
                                                    start=True, stop=True)
                        last.then_inc(tx_d, 1)
                    else:
                        for c in range(C):
                            last = nc.tensor.matmul(halves(ch(ps[2], c), n, 1), ch(Xs, c), halves(ch(TT, c), n, 1),
                                                    start=True, stop=True)
                        last.then_inc(xt_d, 1)
                return step

            def w():
                pe.wait_ge(tt_d, i * 2)
                for c in range(1, C):
                    last = nc.tensor.matmul(ch(ps[1], c), ch(kb, c), ch(TT, c), start=True, stop=True)
                last.then_inc(w_d, 1)

            def v(c):
                def step():
                    if c == 0:
                        pe.wait_ge(vb_d, i)
                    last = nc.tensor.matmul(ch(ps[3], c), ch(TT, c), ch(vb, c), start=True, stop=(c == 0))
                    if c > 0:
                        if c == 1:
                            pe.wait_ge(nw_d, i)
                        pe.wait_ge(s_d, b * 3 + c)
                        last = nc.tensor.matmul(ch(ps[3], c), ch(nw, c), S, start=False, stop=True)
                    last.then_inc(v_d, 1)
                    if c > 0:
                        if c == 1:
                            pe.wait_ge(qd_d, i)
                        nc.tensor.matmul(ch(ps[5], c), S, ch(qd, c), start=True, stop=False)
                return step

            def os(c):
                def step():
                    pe.wait_ge(vn_d, b * 4 + c + 1)
                    if c < C - 1:
                        nc.tensor.matmul(ps[4][:, 0:P], ch(kd, c), ch(vn, c), start=True, stop=True).then_inc(su_d, 1)
                    if c == 0 and (not isinstance(i, int) or i > 1):
                        pe.wait_ge(o1_d, b)
                    last = nc.tensor.matmul(ch(ps[5], c), ch(vn, c), ch(qkd, c), start=(c == 0), stop=True)
                    if c == C - 1:
                        last.then_inc(o_d, 1)
                return step

            def norm():
                pe.wait_ge(osq_d, i)
                nc.tensor.matmul(ps[4][:], ones, osq, start=True, stop=True).then_inc(oss_d, 1)

            return ([first, level1] + [s for n in range(1, 7) for s in (x(n), tx(n))]
                    + [w] + [s for c in range(C) for s in (v(c), os(c))] + [norm])

        def pe_kq_norm(pe, i, n):
            if n == 0 and (not isinstance(i, int) or i > 0):
                pe.wait_ge(nw_d, i)
                pe.wait_ge(tt_d, i * 2)
            pe.wait_ge(ksq_d, i * 2 + n + 1)
            nc.tensor.matmul(ps[1 + n][:], ones, (sk, sq)[n], start=True, stop=True).then_inc(kss_mm, 1)

        FILL = [5, 2, 2, 1, 2, 1, 2, 1, 2, 1, 2, 1, 2, 1, 0, 1, 1, 1, 1, 0, 1, 0, 1, 1]
        KQ_AT = {18: 0, 19: 1}
        assert sum(FILL) == 4 * KT
        OUT_AHEAD = ((4, 5), (5,), (5,), (), (), (), (2,), (2,))
        LAST_FILL = [3, 2, 2, 0, 2, 0, 1, 0, 1, 0, 1, 0, 1, 1, 1, 1, 1, 1, 1, 1, 1, 1, 2, 4]
        assert sum(LAST_FILL) == 4 * (KT - 1)

        def pe_out_steps(pe):
            pe.wait_ge(yl_d, H - 2)
            units = [unit_steps(pe, Unit(U_OUT1 + n), yh, yl) for n in range(4)]
            for unit in units[:2]:
                for _ in range(KT - 2):
                    next(unit)
                    yield
            pe.wait_ge(yl_d, H - 1)
            for unit in units[:2]:
                next(unit)
                yield
            for unit in units[2:]:
                pe.wait_ge(tt_d, H * 2)
                for _ in range(KT - 1):
                    next(unit)
                    yield
            pe.wait_ge(yl_d, H)
            for unit in units:
                for _ in unit:
                    pass
            yield

        def pe_gdn(pe, i, head, project, out_steps=None):
            def units():
                for n in range(4):
                    if not head:
                        yield from unit_steps(pe, Unit(n), yh, yl, x_gate if n == 0 else None)
                    else:
                        if n == 0 and isinstance(i, int):
                            pe.wait_ge(xl_done, KT)
                        yield from unit_steps(pe, Unit(n, i, 4), xh, xl)
            todo = units()

            def x_gate(k):
                pe.wait_ge(x_lo, k + 1)
            if head:
                for at, step in enumerate(pe_head_steps(pe, i)):
                    step()
                    if project:
                        for _ in range(FILL[at]):
                            next(todo)
                        if at in KQ_AT:
                            pe_kq_norm(pe, i, KQ_AT[at])
                    else:
                        for _ in range(LAST_FILL[at]):
                            next(out_steps)
            else:
                gates = dict(zip((8, 13, 22, 27), pe_gate_steps(pe)))
                for n in range(4 * KT):
                    if n in gates:
                        gates[n]()
                    next(todo)
                    if n == KT - 1:
                        pe.wait_ge(s_keep, 16)
                        pe.wait_ge(x_sq, KT - 1)
                        nc.tensor.matmul(ps[0][:], ones, accb, start=True, stop=True).then_inc(rs_mm, 1)
                    if n == 4 * KT - 2:
                        pe_kq_norm(pe, i, 0)
                        pe_kq_norm(pe, i, 1)
            if project:
                for _ in todo:
                    pass

        def pe_mlp(pe, base, g, x0, first, freed=None):
            for n in range(KT):
                u = Unit(base + n, g, 16)
                if first and n == 0:
                    def gate(k):
                        pe.wait_ge(xl_done, x0 + k + 1)
                    run_unit(pe, u, xh, xl, gate)
                    rstd_mm(pe, x0)
                else:
                    run_unit(pe, u, xh, xl)
            for n in range(KT):
                u = Unit(base + KT + n, g, 16)
                gate = None
                if n == 0:
                    def gate(k):
                        pe.wait_ge(yl_done, hid_count(base, g) + k + 1)
                run_unit(pe, u, yh, yl, gate, freed=freed if n == KT - 1 else None)

        def hid_count(base, g):
            return (0 if base == U_FF1 else FF_GROUPS * KT) + g * KT

        def rstd_mm(pe, sums):
            pe.wait_ge(accs_t, sums)
            nc.tensor.matmul(ps[0][:], ones, accb, start=True, stop=True).then_inc(rs_mm, 1)

        accb, rstd = W(27), W(28)
        yl_done = sem("hidden_split")
        hid_sq, hid_h = sem("hidden_squared"), sem("hidden_hi")

        def pe_pair_steps(pe, i):
            b = i - 1
            past = not isinstance(i, int) or i > 1

            def vtok():
                u = Unit(U_ATT - 4 + 2, i, 4)
                pe.wait_ge(evac[u.const % 2], u.half(1))
                pe.wait_ge(qk_ln, i * 2)
                for c in range(C):
                    last = nc.tensor.transpose(ch(ps[4], c), ch(vr, c), ident)
                last.then_inc(vt_mm, 1)

            def scores(n):
                rows_ = slice(HD * n, HD * (n + 1))

                def step():
                    if n == 0:
                        pe.wait_ge(qk_n, i * 2)
                    if n > 0 or past:
                        pe.wait_ge(aw_d, b * 2 + n)
                    for kb, (z, at, _) in enumerate(ZAT):
                        nc.tensor.matmul(ps[z][:, at:at + T - kb * P], ch(kn, kb)[rows_, :], qn[rows_, kb * P:],
                                         start=(kb < 3), stop=False, skip_group_check=True)
                    for kb, (z, at, _) in enumerate(ZAT):
                        last = nc.tensor.matmul(ps[z][:, at:at + P], ident_r, negm_r, start=False, stop=False,
                                                skip_group_check=True)
                    last.then_inc(z_d, 1)
                return step

            def suffix(n):
                def step():
                    for part, ready in ((sph, sh_d), (spl, sl_d)):
                        pe.wait_ge(ready, (b * 2 + n + 1) * 3)
                        for kb, (z, at, _) in enumerate(ZAT):
                            for k2 in range(kb, C):
                                z2, at2, _ = ZAT[k2]
                                last = nc.tensor.matmul(ps[z][:, at + (k2 - kb) * P:at + T - kb * P],
                                                        ntri_r if k2 == kb else nones_r,
                                                        part[z2][:, at2:at2 + T - k2 * P],
                                                        start=False, stop=(part is spl and k2 == C - 1),
                                                        skip_group_check=True)
                    last.then_inc(lw_d, 1)
                return step

            def attend(n):
                def step():
                    pe.wait_ge(aw_d, b * 2 + n + 1)
                    if n == 0:
                        pe.wait_ge(vt_d, i)
                        if past:
                            pe.wait_ge(al_d, b)
                    for kb, (_, _, at) in enumerate(ZAT):
                        last = nc.tensor.matmul(ps[3][HD * n:HD * (n + 1), kb * P:], ch(vt, kb)[:, HD * n:HD * (n + 1)],
                                                aw[:, at:at + T - kb * P], start=(kb == 0), stop=(kb == C - 1))
                    last.then_inc(av_d, 1)
                return step

            return [vtok, scores(0), suffix(0), attend(0), scores(1), suffix(1), attend(1)]

        def pe_qk_sum(pe, i, n):
            pe.wait_ge(qk_sq, i * 2 + n + 1)
            if not isinstance(i, int) or i > 0:
                pe.wait_ge(qk_ln, i * 2)
                pe.wait_ge(vt_d, i)
            nc.tensor.matmul(ps[5 - n][:], blk, (qs, ks)[n], start=True, stop=True).then_inc(qk_sum, 1)

        def pe_proj(pe, n):
            u = U_PLE + n
            pe.wait_ge(lo_done, u + 1)
            if n == 0:
                pe.wait_ge(p_lo, 1)
            else:
                pe.wait_ge(evac[(u - 1) % 2], (u - 1) // 2 + 1)
            for m in range(4):
                for k in range(2):
                    hi, lo = ch(wh[u % 4], k * 4 + m), ch(wl[u % 4], k * 4 + m)
                    nc.tensor.matmul(ps[2 + m][:], hi, ph[:, k, :], start=(k == 0), stop=False)
                    nc.tensor.matmul(ps[2 + m][:], hi, pl[:, k, :], start=False, stop=False)
                    mm = nc.tensor.matmul(ps[2 + m][:], lo, ph[:, k, :], start=False, stop=(k == 1))
                mm.then_inc(unit_done if m == 3 else ple_mm, 1)

        ATT_FILL = [0, 10, 3, 0, 10, 3, 6]

        def pe_att(pe, i, head, project):
            normed = not (isinstance(i, int) and i == PAIRS)
            if not head:
                pe.wait_ge(s_cst, 32)

                def gate(k):
                    pe.wait_ge(xl_done, 2 * KT + k + 1)
                pe_proj(pe, 0)
                pe.wait_ge(accs_t, 2 * KT)
                nc.tensor.matmul(ps[0][:], ones, accb, start=True, stop=True).then_inc(rs2_mm, 1)
                pe.wait_ge(sums2, KT)
                nc.tensor.matmul(ps[1][:], ones, sum2, start=True, stop=True).then_inc(rs2_mm, 1)
                pe_proj(pe, 1)
                run_unit(pe, Unit(U_ATT), xh, xl, gate)
                run_unit(pe, Unit(U_ATT + 1), xh, xl)
                run_unit(pe, Unit(U_ATT + 2), xh, xl)
                pe_qk_sum(pe, i, 0)
                pe_qk_sum(pe, i, 1)
                run_unit(pe, Unit(U_ATT + 3), xh, xl)
                pe.wait_ge(tri_d, 2)
                return

            def units():
                for n in range(4):
                    yield from unit_steps(pe, Unit(U_ATT + n, i, 4), xh, xl)
            todo, done = units(), 0
            for at, step in enumerate(pe_pair_steps(pe, i)):
                step()
                for _ in range(ATT_FILL[at]):
                    next(todo)
                    done += 1
                    if normed and done in (16, 24):
                        pe_qk_sum(pe, i, done // 8 - 2)
            for _ in todo:
                pass

        def pe_conv_sgu(pe):
            for t in range(2):
                pe.wait_ge(sg_sq, t + 1)
                nc.tensor.matmul(ps[5 - t][:], blk, (qs, ks)[t], start=True, stop=True).then_inc(sg_sum, 1)
            run_unit(pe, Unit(U_CONV + 4), xh, xl)
            for t in range(2):
                pe.wait_ge(sg_n, t + 1)
                for c in range(C):
                    last = nc.tensor.transpose(ch(ps[t], c), ch((qn, kn)[t], c), ident)
                last.then_inc(sg_tr, 1)
            last_unit = unit_steps(pe, Unit(U_CONV + 5), xh, xl)
            for _ in range(KT // 2):
                next(last_unit)
            pe.wait_ge(al_d, PAIRS)
            pe.wait_ge(sg_w, 1)
            for t in range(2):
                pe.wait_ge(sg_cp[t], 1)
                for n in range(2):
                    for c in range(C):
                        last = nc.tensor.matmul(ps[2 + t][HD * n:HD * (n + 1), c * P:(c + 1) * P],
                                                ch(vtok[t], c)[:, HD * n:HD * (n + 1)], ch(wsT, 2 * t + n),
                                                start=True, stop=True)
                last.then_inc(sg_mm, 1)
            for _ in last_unit:
                pass

        def mixed_gate(k):
            if k < 2:
                nc.tensor.wait_ge(y_lo, (1, 4)[k])
            elif k == 2:
                nc.tensor.wait_ge(al_d, PAIRS)
            elif k >= 6:
                nc.tensor.wait_ge(y_lo, k - 4)

        def pe_final(pe):
            for n in range(KT):
                def gate(k):
                    pe.wait_ge(xl_done, 4 * KT + k + 1)
                run_unit(pe, Unit(U_GATE + n), xh, xl, gate if n == 0 else None)
                if n == 0:
                    rstd_mm(pe, 4 * KT)

        @block.tensor
        def _(pe):
            pe_gdn(pe, 0, False, True)
            pe_gdn(pe, 1, True, True)
            with pe.Fori(2, H) as i:
                pe_gdn(pe, i, True, True)
            out_steps = pe_out_steps(pe)
            pe_gdn(pe, H, True, False, out_steps)
            next(out_steps)
            for n in range(4, KT):
                run_unit(pe, Unit(U_OUT1 + n), yh, yl)
            pe_mlp(pe, U_FF1, 0, KT, True)
            with pe.Fori(1, FF_GROUPS - 1) as g:
                pe_mlp(pe, U_FF1, g, 0, False)
            pe_mlp(pe, U_FF1, FF_GROUPS - 1, 0, False, freed=y_free)
            pe_att(pe, 0, False, True)
            pe_att(pe, 1, True, True)
            with pe.Fori(2, PAIRS) as i:
                pe_att(pe, i, True, True)
            pe_att(pe, PAIRS, True, True)
            pe_conv_sgu(pe)
            order = (2, 3, 4, 5, 6, 7, 0, 1)
            firsts = [unit_steps(pe, Unit(U_OUT2 + n), yh, yl, mixed_gate, order) for n in range(2)]
            for unit in firsts:
                for _ in range(4):
                    next(unit)
            for unit in firsts:
                for _ in unit:
                    pass
            for n in range(2, KT):
                run_unit(pe, Unit(U_OUT2 + n), yh, yl)
            pe_mlp(pe, U_FF2, 0, 3 * KT, True)
            with pe.Fori(1, FF_GROUPS) as g:
                pe_mlp(pe, U_FF2, g, 0, False)
            pe_final(pe)

        def act_rstd(act, n, src, dst, scale):
            act.wait_ge(rs_mm, n)
            nc.scalar.activation(dst, src, ACT.Ln, scale=scale, bias=EPS).then_inc(lnd, 1)
            act.wait_ge(lnd, n)
            nc.scalar.activation(dst, dst, ACT.Exp, scale=-0.5).then_inc(rst, 1)

        def act_gate_steps(act):
            def s1():
                act.wait_ge(g_dve, 4)
                nc.scalar.activation(small[:, 64:96], small[:, 0:32], ACT.Abs).then_inc(g_act, 1)
                act.wait_ge(g_act, 2)
                nc.scalar.activation(small[:, 64:96], small[:, 64:96], ACT.Exp, scale=-1.0).then_inc(g_act, 1)
                act.wait_ge(g_act, 3)
                nc.scalar.activation(small[:, 64:96], small[:, 64:96], ACT.Ln, bias=1.0).then_inc(g_act, 1)
                nc.scalar.activation(small[:, 128:160], small[:, 32:64], ACT.Exp, scale=-1.0).then_inc(g_act, 1)
                nc.scalar.activation(small[:, 160:168], par[:, PC["a_log"][0]:PC["a_log"][1]], ACT.Exp).then_inc(g_act, 1)

            def s2():
                act.wait_ge(g_dve, 8)
                nc.scalar.activation(tabs[:, 64:96], tabs[:, 0:32], ACT.Exp).then_inc(g_act, 1)
                nc.scalar.activation(tabs[:, 96:160], tabs[:, 96:160], ACT.Exp).then_inc(g_act, 1)

            def s3():
                act.wait_ge(g_dve, 10)
                act.dma_start(rows.rearrange("s c h t -> (s c h) t"), W(23)[0:64, 0:P]).then_inc(g_dma, 16)
            return s1, s2, s3

        def act_rows(act, i):
            for s, dst in ((0, grow), (1, brow)):
                src = rows[s][:, bass.ds(i, 1), :].rearrange("c a t -> (c a) t").partition_broadcast(P)
                act.dma_start(c3(dst), src).then_inc(rows_in, 16)

        def act_gdn(act, i, head, project):
            b = i - 1
            nonfirst = not isinstance(i, int) or i > 0

            def xcopy(n):
                act.wait_ge(x_d, b * 6 + n)
                if n > 1:
                    act.wait_ge(tx_d, b * 5 + n - 1)
                elif not isinstance(i, int) or i > 1:
                    act.wait_ge(xt_d, b * 6)
                nc.scalar.activation(Xs, ps[0][:], ACT.Copy).then_inc(xs_d, 1)
                if n > 1:
                    act.wait_ge(xt_d, b * 6 + n - 1)
                    nc.scalar.activation(halves(TT, n - 1, 1), halves(ps[2][:], n - 1, 1), ACT.Copy).then_inc(tc_d, 1)

            def take(n, split=True):
                u = Unit(n, i, 4)
                if split:
                    split_hi(act, u.plus(2))
                act.wait_ge(unit_done, u.number(1))
                if n < 3:
                    if n > 0 or nonfirst:
                        act.wait_ge(conv_st, i * 12 + 4 * n)
                    else:
                        act.wait_ge(zp, 1)
                    nc.scalar.activation(xpad[:, 3:3 + T], acc[u.const % 2][:], ACT.Copy).then_inc(evac[u.const % 2], 1)
                else:
                    nc.scalar.activation(graw, acc[u.const % 2][:], ACT.Copy).then_inc(evac[u.const % 2], 1)

            def normed(first, last):
                for k in range(first, last):
                    act.wait_ge(xr_d, k + 1)
                    nc.scalar.activation(xh[:, k, :], W(11 + k), ACT.Copy, scale=pc("mix_g", k)).then_inc(xh_done, 1)

            if head:
                act.wait_ge(darg_d, i)
                nc.scalar.activation(dec, dec, ACT.Exp).then_inc(dec_d, 1)
                split_hi(act, Unit(1, i, 4))
                if not isinstance(i, int) or i > 1:
                    act.wait_ge(unit_done, Unit(-1, i, 4).number(1))
                    nc.scalar.activation(graw, acc[1][:], ACT.Copy).then_inc(evac[1], 1)
                if not isinstance(i, int) or i > 1:
                    act.wait_ge(qd_d, b)
                act.wait_ge(rows_in, i * 32)
                nc.scalar.activation(eg, grow, ACT.Exp).then_inc(eg_d, 1)
                xcopy(1)
                if project:
                    take(0)
                xcopy(2)
                xcopy(3)
                if project:
                    take(1)
                xcopy(4)
                xcopy(5)
                if project:
                    split_hi(act, Unit(4, i, 4))
                else:
                    for n in range(2, 4):
                        split_hi(act, Unit(U_OUT1 + n))
                xcopy(6)
                if project:
                    take(2, split=False)
                    act.wait_ge(lt_d, i)
                    act.wait_ge(eg_d, i)
                    act_rows(act, i)
            else:
                s1, s2, s3 = act_gate_steps(act)
                split_hi(act, Unit(2))
                act.wait_ge(g_pe, 1)
                split_hi(act, Unit(3))
                normed(0, 3)
                s1()
                split_hi(act, Unit(4))
                s2()
                normed(3, KT)
            if project:
                if head:
                    act_nw(act, i)
                    act_gs(act, i)
                act.wait_ge(conv_st, i * 12 + 4)
                nc.scalar.activation(kc, kc, ACT.Silu).then_inc(silu_d, 1)
                act.wait_ge(conv_st, i * 12 + 8)
                nc.scalar.activation(qc, qc, ACT.Silu).then_inc(silu_d, 1)
                act.wait_ge(silu_d, i * 4 + 2)
                nc.scalar.activation(sk, kc, ACT.Square).then_inc(ksq_d, 1)
                nc.scalar.activation(sq, qc, ACT.Square).then_inc(ksq_d, 1)
                if not head:
                    s3()
                act.wait_ge(conv_st, i * 12 + 12)
                nc.scalar.activation(vc, vc, ACT.Silu).then_inc(silu_d, 1)
            else:
                act_nw(act, i)
                act_gs(act, i)
            act.preload_act_table_set(LN_EXP)
            if project:
                for n, buf in enumerate((sk, sq)):
                    act.wait_ge(kss_mm, i * 2 + n + 1)
                    nc.scalar.activation(buf, ps[1 + n][:], ACT.Ln, bias=EPS).then_inc(kln, 1)
                for n, buf in enumerate((sk, sq)):
                    act.wait_ge(kln, i * 2 + n + 1)
                    nc.scalar.activation(buf, buf, ACT.Exp, scale=-0.5).then_inc(krs, 1)
                if not head:
                    act.wait_ge(g_dma, 16)
                    act_rows(act, i)
            if head:
                act.wait_ge(o_d, i)
                nc.scalar.activation(osq, ps[5][:], ACT.Square).then_inc(osq_d, 1)
                act.wait_ge(oss_d, i)
                nc.scalar.activation(osq, ps[4][:], ACT.Ln, scale=1.0 / P, bias=EPS).then_inc(oln, 1)
                act.wait_ge(oln, i)
                nc.scalar.activation(osq, osq, ACT.Exp, scale=-0.5).then_inc(ors, 1)
        def act_nw(act, i):
            act.wait_ge(w_d, i)
            nc.scalar.activation(nw[:, P:], ps[1][:, P:], ACT.Copy, scale=-1.0).then_inc(nw_d, 1)

        def act_gs(act, i):
            if not isinstance(i, int) or i > 1:
                act.wait_ge(yb_d, i - 1)
            act.wait_ge(evac[1], i * 2)
            nc.scalar.activation(gs, graw, ACT.Silu).then_inc(silu_d, 1)

        act_nrm = [KT]

        def act_norm_tile(act, m, b, half, gname):
            n = act_nrm[0]
            act_nrm[0] += 1
            act.wait_ge(evac[b], half)
            nc.scalar.activation(xh[:, m, :], h[:, m, :], ACT.Copy, scale=pc(gname, m)).then_inc(xh_done, 1)
            if n > KT:
                act.wait_ge(accs_t, n - KT)
            nc.scalar.activation(W(26), h[:, m, :], ACT.Square).then_inc(sqs, 1)
            if gname == "fn_g":
                if m > 0:
                    act.wait_ge(sums2, m)
                nc.scalar.activation(sq2, h[:, m, :], ACT.Square, scale=pc("fin_g", m)).then_inc(sqs2, 1)

        def act_mlp(act, base, g, first, last, gname):
            for n in range(KT):
                u = Unit(base + n, g, 16)
                split_hi(act, u.plus(2))
                if first and n == 0:
                    act_rstd(act, 2 if base == U_FF1 else 3, ps[0][:], rstd, 1.0 / D)
                cnt = hid_count(base, g) + n
                act.wait_ge(evac[u.const % 2], u.half(1))
                if not isinstance(cnt, int) or cnt > 0:
                    act.wait_ge(yl_done, cnt)
                nc.scalar.activation(hs, hr, ACT.Square).then_inc(hid_sq, 1)
                act.wait_ge(hid_sq, cnt + 1)
                nc.scalar.activation(yh[:, n, :], hs, ACT.Copy).then_inc(hid_h, 1)
            for n in range(KT):
                u = Unit(base + KT + n, g, 16)
                if exists(u.plus(2)):
                    split_hi(act, u.plus(2))
                if last and base == U_FF1 and n == KT - 1:
                    act.wait_ge(p_in, 16)
                    act.wait_ge(y_free, 1)
                    nc.scalar.activation(ph, praw, ACT.Copy).then_inc(p_hi, 1)
                if last:
                    act_norm_tile(act, n, u.const % 2, u.half(1), gname)

        hr, hs = W(24), W(25)

        def act_rsqrt(act, buf, src, scale, summed, summed_n, ln_sem, rs_sem, n):
            act.wait_ge(summed, summed_n)
            nc.scalar.activation(buf, src, ACT.Ln, scale=scale, bias=EPS).then_inc(ln_sem, 1)
            act.wait_ge(ln_sem, n)
            nc.scalar.activation(buf, buf, ACT.Exp, scale=-0.5).then_inc(rs_sem, 1)

        def act_proj(act, n):
            u = U_PLE + n
            split_hi(act, Unit(u + 2))
            if n == 1:
                act.wait_ge(p_lo, 1)
            for m in range(4):
                if m < 3:
                    act.wait_ge(ple_mm, 3 * n + m + 1)
                else:
                    act.wait_ge(unit_done, u + 1)
                nc.scalar.activation(ch5(stage[n], m), ps[2 + m][:], ACT.Copy).then_inc(ple_cp if m < 3 else evac[u % 2], 1)
            act.wait_ge(ple_cp, 3 * n + 3)
            act.wait_ge(evac[u % 2], u // 2 + 1)
            act.dma_start(proj[:, 4 * n:4 * n + 4, :], stage[n].rearrange("p (k t) -> p k t", t=T)).then_inc(pp_out[n], 16)

        def act_att(act, i, head, project):
            b = i - 1
            past = not isinstance(i, int) or i > 1
            normed = not (isinstance(i, int) and i == PAIRS)

            def hi(n):
                split_hi(act, Unit(U_ATT + n + 2, i, 4))

            def soft(n):
                act.wait_ge(z_d, b * 2 + n + 1)
                if n > 0 or past:
                    act.wait_ge(sp_d, (b * 2 + n) * 3)
                for z, (at, w) in enumerate(ZBANK):
                    last = nc.scalar.activation(az[:, at:at + w], ps[z][:, 0:w], ACT.Abs)
                last.then_inc(abs_d, 1)
                act.wait_ge(abs_d, b * 2 + n + 1)
                nc.scalar.activation(az, az, ACT.Exp, scale=-1.0).then_inc(ez_d, 1)
                act.wait_ge(ez_d, b * 2 + n + 1)
                for at, w in ZBANK:
                    nc.scalar.activation(az[:, at:at + w], az[:, at:at + w], ACT.Ln, bias=1.0).then_inc(lz_d, 1)
                for z, (at, w) in enumerate(ZBANK):
                    act.wait_ge(sp_d, (b * 2 + n) * 3 + z + 1)
                    nc.scalar.activation(sph[z][:, 0:w], spz[:, at:at + w], ACT.Copy).then_inc(sh_d, 1)

            def weights(n):
                act.wait_ge(lw_d, b * 2 + n + 1)
                if n > 0 or past:
                    act.wait_ge(av_d, b * 2 + n)
                for z, (at, w) in enumerate(ZBANK):
                    last = nc.scalar.activation(aw[:, at:at + w], ps[z][:, 0:w], ACT.Exp)
                last.then_inc(aw_d, 1)

            def square(n):
                u = Unit(U_ATT + n, i, 4)
                act.wait_ge(evac[u.const % 2], u.half(1))
                if head:
                    act.wait_ge(qk_n, i * 2)
                nc.scalar.activation((qs, ks)[n], (qr, kr)[n], ACT.Square).then_inc(qk_sq, 1)

            def rsqrt(n):
                act_rsqrt(act, (qs, ks)[n], ps[5 - n][:], 1.0 / HD, qk_sum, i * 2 + n + 1, qk_ln, qk_rs, i * 2 + n + 1)

            if not head:
                act_proj(act, 0)
                act_rsqrt(act, rf, ps[0][:], 1.0 / D, rs2_mm, 1, ln2, rs2, 1)
                act_proj(act, 1)
                hi(0)
                act_rsqrt(act, r1, r1, 1.0 / D, scale_d, 2, ln2, rs2, 2)
                hi(1)
                square(0)
                square(1)
                hi(2)
                rsqrt(0)
                rsqrt(1)
                hi(3)
                act.wait_ge(pp_out[1], 16)
                act.wait_ge(s_cst, 32)
                nc.scalar.activation(yh[:, 7, 0:3 * P], cst[:, 0:3 * P], ACT.Copy).then_inc(tri_d, 1)
                nc.scalar.activation(yh[:, 7, 3 * P:], ident, ACT.Copy).then_inc(tri_d, 1)
                return
            hi(0)
            act.wait_ge(vt_mm, i)
            if past:
                act.wait_ge(av_d, b * 2)
            nc.scalar.activation(vt, ps[4][:], ACT.Copy).then_inc(vt_d, 1)
            soft(0)
            hi(1)
            weights(0)
            if normed:
                square(0)
            soft(1)
            if normed:
                square(1)
                rsqrt(0)
            hi(2)
            weights(1)
            if normed:
                rsqrt(1)
            hi(3)

        def act_conv_sgu(act):
            for t in range(4):
                u = U_ATT + 4 * PAIRS - 1
                act.wait_ge(evac[u % 2], u // 2 + 1)
                nc.scalar.activation(ch5(uv, t), ch5(uv, t), ACT.Gelu).then_inc(gelu_d, 1)
            for t in range(2):
                act.wait_ge(gelu_d, 3 + t)
                nc.scalar.activation((qs, ks)[t], ch5(uv, 2 + t), ACT.Square).then_inc(sg_sq, 1)
            split_hi(act, Unit(U_CONV + 6))
            act.preload_act_table_set(LN_EXP)
            for t in range(2):
                act_rsqrt(act, (qs, ks)[t], ps[5 - t][:], 1.0 / HD, sg_sum, t + 1, sg_ln, sg_rs, t + 1)
            act.wait_ge(cv, 5)
            nc.scalar.activation(yh[:, 0, :], qr, ACT.Copy).then_inc(y_hi, 1)
            act.wait_ge(sg_tr, 1)
            nc.scalar.activation(vtok[0], ps[0][:], ACT.Copy).then_inc(sg_cp[0], 1)
            split_hi(act, Unit(U_CONV + 7))
            for t in range(2):
                act.wait_ge(sg_y, t + 1)
                nc.scalar.activation(yh[:, 6 + t, :], sgy[t], ACT.Copy).then_inc(y_hi, 1)
            act.wait_ge(cv, 10)
            nc.scalar.activation(yh[:, 1, :], kr, ACT.Copy).then_inc(y_hi, 1)

        def act_final(act):
            act_rstd(act, 4, ps[0][:], rstd, 1.0 / D)
            for n in range(KT):
                u = Unit(U_GATE + n)
                if exists(u.plus(2)):
                    split_hi(act, u.plus(2))
                act.wait_ge(evac[u.const % 2], u.half(1))
                nc.scalar.activation(gz[n % 2], gz[n % 2], ACT.Sigmoid).then_inc(gate_s, 1)

        @block.scalar
        def _(act):
            act.preload_act_table_set(LN_EXP)
            split_hi(act, Unit(0))
            act.wait_ge(s_par, 16)
            for k in range(KT):
                if k % 2 == 0:
                    act.wait_ge(s_x[k // 2], 16)
                nc.scalar.activation(yh[:, k, :], h[:, k, :], ACT.Copy, scale=pc("mix_g", k)).then_inc(x_hi, 1)
                nc.scalar.activation(W(11 + k), h[:, k, :], ACT.Square).then_inc(sqs, 1)
            act.wait_ge(s_wab, 16)
            nc.scalar.activation(wh[3][:, 0:P], W(21)[:, 0:P], ACT.Copy).then_inc(g_act, 1)
            split_hi(act, Unit(1))
            act_rstd(act, 1, ps[0][:], W(20), 1.0 / D)
            act_gdn(act, 0, False, True)
            act_gdn(act, 1, True, True)
            with act.Fori(2, H) as i:
                act_gdn(act, i, True, True)
            act_gdn(act, H, True, False)
            for n in range(KT):
                u = Unit(U_OUT1 + n)
                for ahead in OUT_AHEAD[n]:
                    split_hi(act, u.plus(ahead))
                act_norm_tile(act, n, u.const % 2, u.half(1), "mlp_g")
            act_mlp(act, U_FF1, 0, True, False, None)
            with act.Fori(1, FF_GROUPS - 1) as g:
                act_mlp(act, U_FF1, g, False, False, None)
            act_mlp(act, U_FF1, FF_GROUPS - 1, False, True, "fn_g")
            act_att(act, 0, False, True)
            act_att(act, 1, True, True)
            with act.Fori(2, PAIRS) as i:
                act_att(act, i, True, True)
            act_att(act, PAIRS, True, True)
            act_conv_sgu(act)
            for n in range(KT):
                u = Unit(U_OUT2 + n)
                split_hi(act, u.plus(2))
                act_norm_tile(act, n, u.const % 2, u.half(1), "n2_g")
            act_mlp(act, U_FF2, 0, True, False, None)
            with act.Fori(1, FF_GROUPS - 1) as g:
                act_mlp(act, U_FF2, g, False, False, None)
            act_mlp(act, U_FF2, FF_GROUPS - 1, False, True, "n3_g")
            act_final(act)

        @block.gpsimd
        def _(pool):
            for k in range(1, KT):
                pool.wait_ge(sqs, k + 1)
                if k > 1:
                    pool.wait_ge(x_sq, k - 1)
                nc.gpsimd.tensor_tensor(accb, W(11) if k == 1 else accb, W(11 + k), ALU.add).then_inc(x_sq, 1)
            pool.wait_ge(rst, 1)
            for k in range(KT):
                nc.gpsimd.tensor_tensor(W(11 + k), h[:, k, :], W(20), ALU.mult).then_inc(xr_d, 1)
            pool.wait_ge(s_cst, 16)

            def masks(i):
                b = i - 1
                pool.wait_ge(lt_d, i)
                for n in range(1, LEVELS):
                    if n == 1 and (not isinstance(i, int) or i > 1):
                        pool.wait_ge(x_d, b * 6)
                    if n == 2:
                        pool.wait_ge(tt_d, b * 2 + 1)
                        pool.wait_ge(l1_d, i)
                    if n > 2:
                        pool.wait_ge(x_d, b * 6 + n - 2)
                    nc.gpsimd.tensor_tensor(c3(Mb[n % 2]), c3(Lt), over_chunks(ch(cst, n)), ALU.mult).then_inc(m_d, 1)
            masks(1)
            with pool.Fori(2, H + 1) as i:
                masks(i)

        def dve_gate_steps(dve):

            def s1():
                dve.wait_ge(g_pe, 1)
                nc.vector.tensor_tensor(W(22)[0:16, :], ps[1][0:16, :], W(20)[0:16, :], ALU.mult).then_inc(g_dve, 1)

            def s2():
                dve.wait_ge(g_pe, 2)
                src = ps[2][:, 0:64].rearrange("p (c x h) -> p x c h", x=2, c=C)
                dtb = par[:, PC["dt_b"][0]:PC["dt_b"][1]].unsqueeze(1).broadcast_to([P, C, H])
                nc.vector.tensor_tensor(small[:, 0:32].rearrange("p (c h) -> p c h", c=C), src[:, 0], dtb,
                                        ALU.add).then_inc(g_dve, 1)
                nc.vector.tensor_copy(small[:, 32:64].rearrange("p (c h) -> p c h", c=C), src[:, 1]).then_inc(g_dve, 1)
                dve.wait_ge(g_act, 6)
                nc.vector.scalar_tensor_tensor(out=small[:, 64:96], in0=small[:, 0:32], scalar=0.0, in1=small[:, 64:96],
                                               op0=ALU.max, op1=ALU.add).then_inc(g_sp, 1)
                dve.wait_ge(g_sp, 1)
                ea = small[:, 160:168].unsqueeze(1).broadcast_to([P, C, H])
                nc.vector.scalar_tensor_tensor(out=small[:, 96:128].rearrange("p (c h) -> p c h", c=C),
                                               in0=small[:, 64:96].rearrange("p (c h) -> p c h", c=C), scalar=-1.0, in1=ea,
                                               op0=ALU.mult, op1=ALU.mult).then_inc(g_dve, 1)
                nc.vector.tensor_scalar(small[:, 128:160], small[:, 128:160], 1.0, None, ALU.add).then_inc(g_sp, 1)
                dve.wait_ge(g_sp, 2)
                nc.vector.reciprocal(tabs[:, 32:64], small[:, 128:160]).then_inc(g_dve, 1)
                dve.wait_ge(g_pe, 3)
                nc.vector.tensor_copy(tabs[:, 0:32], ps[3][:, 0:32]).then_inc(g_dve, 1)
                nc.vector.tensor_copy(tabs[:, 128:160], ps[3][:, 32:64]).then_inc(g_sp, 1)
                dve.wait_ge(g_sp, 3)
                dve.wait_ge(g_dve, 7)
                nc.vector.tensor_tensor(tabs[:, 96:128], tabs[:, 128:160], tabs[:, 0:32], ALU.subtract).then_inc(g_dve, 1)

            def s3():
                dve.wait_ge(g_act, 8)
                nc.vector.tensor_tensor(tabs[:, 64:96], tabs[:, 64:96], tabs[:, 32:64], ALU.mult).then_inc(g_dve, 1)
                dve.wait_ge(g_pe, 4)
                dve.wait_ge(g_dve, 9)
                nc.vector.tensor_copy(W(23)[0:64, 0:P], ps[4][0:64, 0:P]).then_inc(g_dve, 1)
            return s1, s2, s3

        g_sp = sem("gate_dve_inner")

        def tc(table, c):
            return tcur[:, table * C + c:table * C + c + 1]

        def dve_gdn(dve, i, head, project):
            b = i - 1

            def cur():
                if head:
                    nc.vector.tensor_copy(tcur.unsqueeze(2), tab5[:, :, bass.ds(b, 1)]).then_inc(cur_done, 1)
                if project:
                    nc.vector.tensor_copy(cwc.unsqueeze(2), cwall[:, :, bass.ds(i, 1)]).then_inc(cur_done, 1)

            def conv_steps(n):
                u = Unit(n, i, 4)
                buf = (kc, qc, vc)[n]
                dve.wait_ge(evac[u.const % 2], u.half(1))
                if n == 0:
                    dve.wait_ge(cur_done, i * 2 + 1)
                sec = (1, 0, 2)[n]

                def tap(j):
                    return cwc[:, sec * TAPS + j:sec * TAPS + j + 1]
                nc.vector.tensor_scalar(buf, xpad[:, 3:3 + T], tap(3), None, ALU.mult).then_inc(conv_st, 1)
                yield
                for j in (2, 1, 0):
                    dve.wait_ge(conv_st, i * 12 + 4 * n + 3 - j)
                    nc.vector.scalar_tensor_tensor(out=buf, in0=xpad[:, j:j + T], scalar=tap(j), in1=buf,
                                                   op0=ALU.mult, op1=ALU.add).then_inc(conv_st, 1)
                    yield

            def conv(n):
                for _ in conv_steps(n):
                    pass

            def upd(n):
                if n < 6:
                    dve.wait_ge(tx_d, b * 5 + n)
                    nc.vector.tensor_tensor(halves(Ti, n, 0), halves(ps[1][:], n, 0), halves(Ti, n, 0), ALU.add).then_inc(t_d, 1)
                else:
                    dve.wait_ge(xt_d, b * 6 + n)
                    nc.vector.tensor_tensor(halves(TT, n, 1), halves(ps[2][:], n, 1), halves(TT, n, 1), ALU.add).then_inc(tt_d, 1)

            def take(n):
                split_lo(dve, Unit(n + 2))
                dve.wait_ge(unit_done, n + 1)
                if n > 0:
                    dve.wait_ge(conv_st, 4 * n)
                nc.vector.tensor_tensor(xpad[:, 3:3 + T], acc[n % 2][:], W(20), ALU.mult).then_inc(evac[n % 2], 1)
                conv(n)

            def normed(first, last):
                for k in range(first, last):
                    dve.wait_ge(xh_done, k + 1)
                    nc.vector.scalar_tensor_tensor(out=xl[:, k, :], in0=W(11 + k), scalar=pc("mix_g", k),
                                                   in1=xh[:, k, :].bitcast(F32), op0=ALU.mult, op1=ALU.subtract).then_inc(xl_done, 1)

            cur()
            if head:
                dve.wait_ge(cur_done, i * 2)
                dve.wait_ge(rows_in, i * 32)
                for c in range(C):
                    ins = nc.vector.tensor_scalar(ch(dec, c), ch(grow, c), tc(0, c), 0.0, ALU.subtract, ALU.min)
                ins.then_inc(darg_d, 1)
                dve.wait_ge(dec_d, i)
                nc.vector.tensor_tensor(c3(dec), c3(dec), over_chunks(tri), ALU.mult).then_inc(dm_d, 1)
                dve.wait_ge(dm_d, i)
                nc.vector.tensor_tensor(Lt, dec, brow, ALU.mult).then_inc(lt1_d, 1)
                dve.wait_ge(lt1_d, i)
                dve.wait_ge(kk_d, i)
                nc.vector.tensor_tensor(Lt, ps[0][:], Lt, ALU.mult).then_inc(lt_d, 1)
                dve.wait_ge(lt_d, i)
                nc.vector.tensor_tensor(c3(Mb[0]), c3(Lt), over_chunks(ch(cst, 0)), ALU.mult).then_inc(m0_d, 1)
                dve.wait_ge(qk_d, i)
                nc.vector.tensor_tensor(qkd, ps[1][:], dec, ALU.mult).then_inc(qkd_d, 1)
                dve.wait_ge(m0_d, i)
                nc.vector.tensor_tensor(c3(TT), c3(Mb[0]), over_chunks(ident), ALU.add).then_inc(tt_d, 1)
                split_lo(dve, Unit(1, i, 4))
                dve.wait_ge(l1_d, i)
                nc.vector.tensor_tensor(c3(Ti), c3(ps[4][:]), over_chunks(ident), ALU.add).then_inc(t_d, 1)
                dve.wait_ge(ktr_d, i)
                for c in range(C):
                    if c < C - 1:
                        nc.vector.tensor_scalar(ch(kd, c), ch(ps[2], c), tc(3, c), None, ALU.mult)
                    if c > 0:
                        ins = nc.vector.tensor_scalar(ch(kb, c), ch(ps[2], c), tc(2, c), None, ALU.mult)
                ins.then_inc(ktok_d, 1)
                if project:
                    split_lo(dve, Unit(2, i, 4))
                upd(1)
                dve.wait_ge(vtr_d, i)
                for c in range(C):
                    ins = nc.vector.tensor_scalar(ch(vb, c), ch(ps[3], c), tc(1, c), None, ALU.mult)
                ins.then_inc(vb_d, 1)
                upd(2)
                if project:
                    conv(0)
                upd(3)
                if not isinstance(i, int) or i > 1:
                    dve_output(dve, b)
                upd(4)
                if project:
                    split_lo(dve, Unit(3, i, 4))
                dve.wait_ge(eg_d, i)
                nc.vector.tensor_tensor(qd[:, P:], qT[:, P:], eg[:, P:], ALU.mult).then_inc(qd_d, 1)
                upd(5)
                if project:
                    conv(1)
                else:
                    split_lo(dve, Unit(U_OUT1 + 2))
                upd(6)
                if not project:
                    split_lo(dve, Unit(U_OUT1 + 3))
                v_taps = conv_steps(2)
                for c in range(C):
                    dve.wait_ge(v_d, b * 4 + c + 1)
                    nc.vector.tensor_copy(ch(vn, c), ch(ps[3], c)).then_inc(vn_d, 1)
                    if c < C - 1:
                        dve.wait_ge(su_d, b * 3 + c + 1)
                        if c == 0:
                            nc.vector.tensor_copy(S, ps[4][:, 0:P]).then_inc(s_d, 1)
                        else:
                            dve.wait_ge(s_d, b * 3 + c)
                            nc.vector.scalar_tensor_tensor(out=S, in0=S, scalar=tc(4, c), in1=ps[4][:, 0:P],
                                                           op0=ALU.mult, op1=ALU.add).then_inc(s_d, 1)
                    if project and c < 2:
                        next(v_taps)
                        next(v_taps)
                if project:
                    split_lo(dve, Unit(4, i, 4))
            else:
                s1, s2, s3 = dve_gate_steps(dve)
                take(0)
                s1()
                take(1)
                s2()
                normed(0, 3)
                take(2)
                s3()
                normed(3, KT)
                dve.wait_ge(unit_done, 4)
                nc.vector.tensor_tensor(graw, acc[1][:], W(20), ALU.mult).then_inc(evac[1], 1)
            if project:
                for n, (dst, src, rs) in enumerate(((kT, kc, sk), (qT, qc, sq))):
                    dve.wait_ge(krs, i * 2 + n + 1)
                    sc = (1.0, float(P) ** -0.5)[n]
                    nc.vector.scalar_tensor_tensor(out=dst, in0=src, scalar=sc, in1=rs, op0=ALU.mult, op1=ALU.mult)\
                      .then_inc(kqn, 1)
        def dve_output(dve, i):
            b = i - 1
            dve.wait_ge(ors, i)
            nc.vector.tensor_tensor(yb, ps[5][:], osq, ALU.mult).then_inc(o1_d, 1)
            dve.wait_ge(o1_d, i)
            dve.wait_ge(silu_d, i * 4)
            nc.vector.scalar_tensor_tensor(out=yb, in0=yb, scalar=pc("onorm_g"), in1=gs, op0=ALU.mult,
                                           op1=ALU.mult).then_inc(yb_d, 1)
            dve.wait_ge(yb_d, i)
            nc.vector.tensor_scalar(yh[:, bass.ds(b, 1), :], yb.unsqueeze(1), 1.0, None, ALU.mult).then_inc(yh_d, 1)
            dve.wait_ge(yh_d, i)
            nc.vector.tensor_tensor(yl[:, bass.ds(b, 1), :], yb.unsqueeze(1),
                                    yh[:, bass.ds(b, 1), :].bitcast(F32), ALU.subtract).then_inc(yl_d, 1)

        tile_n = [KT]

        def dve_stream_tile(dve, m, u, gname):
            b = u.const % 2
            dve.wait_ge(unit_done, u.number(1))
            nc.vector.tensor_tensor(h[:, m, :], accumulator(u)[:], h[:, m, :], ALU.add).then_inc(evac[b], 1)
            if gname is None:
                return
            n = tile_n[0]
            tile_n[0] += 1
            dve.wait_ge(xh_done, n + 1)
            nc.vector.scalar_tensor_tensor(out=xl[:, m, :], in0=h[:, m, :], scalar=pc(gname, m),
                                           in1=xh[:, m, :].bitcast(F32), op0=ALU.mult, op1=ALU.subtract).then_inc(xl_done, 1)
            dve.wait_ge(sqs, n + 1)
            if m == 0:
                ins = nc.vector.tensor_copy(accb, W(26))
            else:
                dve.wait_ge(accs_t, n - KT)
                ins = nc.vector.tensor_tensor(accb, accb, W(26), ALU.add)
            ins.then_inc(accs_t, 1)
            if gname == "fn_g":
                dve.wait_ge(sqs2, m + 1)
                if m == 0:
                    ins = nc.vector.tensor_copy(sum2, sq2)
                else:
                    dve.wait_ge(sums2, m)
                    ins = nc.vector.tensor_tensor(sum2, sum2, sq2, ALU.add)
                ins.then_inc(sums2, 1)

        def dve_mlp(dve, base, g, first, last, gname):
            for n in range(KT):
                u = Unit(base + n, g, 16)
                b = u.const % 2
                split_lo(dve, u.plus(2))
                cnt = hid_count(base, g) + n
                dve.wait_ge(unit_done, u.number(1))
                if first and n == 0:
                    dve.wait_ge(rst, 2 if base == U_FF1 else 3)
                if not isinstance(cnt, int) or cnt > 0:
                    dve.wait_ge(hid_sq, cnt)
                nc.vector.scalar_tensor_tensor(out=hr, in0=acc[b][:], scalar=0.0, in1=rstd, op0=ALU.max,
                                               op1=ALU.mult).then_inc(evac[b], 1)
                dve.wait_ge(hid_h, cnt + 1)
                nc.vector.tensor_tensor(yl[:, n, :], hs, yh[:, n, :].bitcast(F32), ALU.subtract).then_inc(yl_done, 1)
            for n in range(KT):
                u = Unit(base + KT + n, g, 16)
                if exists(u.plus(2)):
                    split_lo(dve, u.plus(2))
                if last and base == U_FF1 and n == KT - 1:
                    dve.wait_ge(p_hi, 1)
                    nc.vector.tensor_tensor(pl, praw, ph.bitcast(F32), ALU.subtract).then_inc(p_lo, 1)
                dve_stream_tile(dve, n, u, gname if last else None)

        def dve_take(dve, i, n, dst):
            u = Unit(U_ATT + n, i, 4)
            dve.wait_ge(unit_done, u.number(1))
            nc.vector.tensor_tensor(dst, acc[u.const % 2][:], tscale, ALU.mult).then_inc(evac[u.const % 2], 1)

        def dve_att(dve, i, head, project):
            b = i - 1
            past = not isinstance(i, int) or i > 1
            normed = not (isinstance(i, int) and i == PAIRS)

            def lo(n):
                split_lo(dve, Unit(U_ATT + n + 2, i, 4))

            def softplus(n):
                if n > 0 or past:
                    dve.wait_ge(sl_d, (b * 2 + n) * 3)
                for z, (at, w) in enumerate(ZBANK):
                    dve.wait_ge(lz_d, (b * 2 + n) * 3 + z + 1)
                    nc.vector.scalar_tensor_tensor(out=spz[:, at:at + w], in0=ps[z][:, 0:w], scalar=0.0,
                                                   in1=az[:, at:at + w], op0=ALU.max, op1=ALU.add).then_inc(sp_d, 1)
                for z, (at, w) in enumerate(ZBANK):
                    dve.wait_ge(sh_d, (b * 2 + n) * 3 + z + 1)
                    nc.vector.tensor_tensor(spl[z][:, 0:w], spz[:, at:at + w], sph[z][:, 0:w].bitcast(F32),
                                            ALU.subtract).then_inc(sl_d, 1)

            def normal(n):
                dve.wait_ge(qk_rs, i * 2 + n + 1)
                if head:
                    dve.wait_ge(z_d, i * 2)
                nc.vector.scalar_tensor_tensor(out=(qn, kn)[n], in0=(qr, kr)[n], scalar=pc(("q_g8", "k_g")[n]),
                                               in1=(qs, ks)[n], op0=ALU.mult, op1=ALU.mult).then_inc(qk_n, 1)

            def gating():
                u = Unit(U_ATT + 3, i, 4)
                dve.wait_ge(unit_done, u.number(1))
                if isinstance(i, int):
                    nc.vector.tensor_tensor(ch5(uv, i), acc[u.const % 2][:], tscale, ALU.mult).then_inc(evac[u.const % 2], 1)
                else:
                    dst = uv.rearrange("p (j t) -> p j t", t=T)[:, bass.ds(i, 1), :]
                    nc.vector.tensor_tensor(dst, acc[u.const % 2][:].unsqueeze(1), tscale.unsqueeze(1), ALU.mult)\
                      .then_inc(evac[u.const % 2], 1)

            if not head:
                split_lo(dve, Unit(U_PLE + 2))
                split_lo(dve, Unit(U_PLE + 3))
                lo(0)
                dve.wait_ge(rs2, 1)
                dve.wait_ge(rs2_mm, 2)
                nc.vector.tensor_tensor(r1, ps[1][:], rf, ALU.mult).then_inc(scale_d, 1)
                dve.wait_ge(scale_d, 1)
                nc.vector.tensor_tensor(r1, r1, rf, ALU.mult).then_inc(scale_d, 1)
                dve.wait_ge(rs2, 2)
                nc.vector.tensor_tensor(tscale, r1, rf, ALU.mult).then_inc(scale_d, 1)
                dve.wait_ge(scale_d, 3)
                dve_take(dve, i, 0, qr)
                lo(1)
                dve_take(dve, i, 1, kr)
                lo(2)
                dve_take(dve, i, 2, vr)
                lo(3)
                normal(0)
                normal(1)
                dve.wait_ge(pp_out[0], 16)
                gating()
                for m in range(KT):
                    nc.vector.scalar_tensor_tensor(out=h[:, m, :], in0=h[:, m, :], scalar=pc("fin_g", m), in1=rf,
                                                   op0=ALU.mult, op1=ALU.mult).then_inc(h_scaled, 1)
                return
            lo(0)
            softplus(0)
            dve_take(dve, i, 0, qr if normed else conv_in[0])
            lo(1)
            dve_take(dve, i, 1, kr if normed else conv_in[1])
            softplus(1)
            lo(2)
            if normed:
                normal(0)
                dve.wait_ge(vt_mm, i)
            dve_take(dve, i, 2, vr if normed else conv_in[2])
            if not normed:
                dve_conv(dve, 0)
            lo(3)
            if normed:
                normal(1)
                gating()
            else:
                dve_take(dve, i, 3, conv_in[3])
            dve.wait_ge(av_d, i * 2)
            nc.vector.tensor_scalar(yh[:, bass.ds(b + 2, 1), :], ps[3][:].unsqueeze(1), 1.0, None, ALU.mult)\
              .then_inc(ah_d, 1)
            dve.wait_ge(ah_d, i)
            nc.vector.tensor_tensor(yl[:, bass.ds(b + 2, 1), :], ps[3][:].unsqueeze(1),
                                    yh[:, bass.ds(b + 2, 1), :].bitcast(F32), ALU.subtract).then_inc(al_d, 1)

        def dve_conv(dve, t):
            ci, hi_, bi = conv_in[3 * t:3 * t + 3]
            dst = (qr, kr)[t]
            last = U_CONV + 3 * t + 2
            for u in (last - 1, last):
                dve.wait_ge(evac[u % 2], u // 2 + 1)
            nc.vector.tensor_tensor(xpad[:, 3:3 + T], ci, hi_, ALU.mult).then_inc(cv, 1)
            dve.wait_ge(cv, 5 * t + 1)
            nc.vector.tensor_scalar(dst, xpad[:, 3:3 + T], pc("conv2_w", 3 * t + 2), None, ALU.mult).then_inc(cv, 1)
            for n, j in enumerate((1, 0)):
                dve.wait_ge(cv, 5 * t + 2 + n)
                nc.vector.scalar_tensor_tensor(out=dst, in0=xpad[:, 1 + j:1 + j + T], scalar=pc("conv2_w", 3 * t + j),
                                               in1=dst, op0=ALU.mult, op1=ALU.add).then_inc(cv, 1)
            dve.wait_ge(cv, 5 * t + 4)
            nc.vector.tensor_tensor(dst, dst, bi, ALU.mult).then_inc(cv, 1)

        def dve_conv_sgu(dve):
            def y_low(n, k, src):
                dve.wait_ge(y_hi, n + 1)
                nc.vector.tensor_tensor(yl[:, k, :], src, yh[:, k, :].bitcast(F32), ALU.subtract).then_inc(y_lo, 1)

            def gate(t):
                dve.wait_ge(sg_mm, t + 1)
                bias = bsT[:, t * P:(t + 1) * P].unsqueeze(1).broadcast_to([P, C, P])
                nc.vector.tensor_tensor(c3(sgy[t]), c3(ps[2 + t][:]), bias, ALU.add).then_inc(sg_b, 1)
                dve.wait_ge(sg_b, t + 1)
                nc.vector.tensor_tensor(sgy[t], sgy[t], ch5(uv, t), ALU.mult).then_inc(sg_y, 1)

            dve.wait_ge(s_cst, 32)
            nc.vector.tensor_tensor(c3(wsT), c3(wsT), over_chunks(tri), ALU.mult).then_inc(sg_w, 1)
            split_lo(dve, Unit(U_CONV + 6))
            for t in range(2):
                dve.wait_ge(sg_rs, t + 1)
                nc.vector.scalar_tensor_tensor(out=(qn, kn)[t], in0=ch5(uv, 2 + t), scalar=pc("sgu_g", t),
                                               in1=(qs, ks)[t], op0=ALU.mult, op1=ALU.mult).then_inc(sg_n, 1)
            dve_take(dve, PAIRS, 4, conv_in[4])
            y_low(0, 0, qr)
            dve.wait_ge(sg_tr, 2)
            nc.vector.tensor_copy(vtok[1], ps[1][:]).then_inc(sg_cp[1], 1)
            split_lo(dve, Unit(U_CONV + 7))
            gate(0)
            gate(1)
            y_low(1, 6, sgy[0])
            y_low(2, 7, sgy[1])
            dve_take(dve, PAIRS, 5, conv_in[5])
            dve_conv(dve, 1)
            y_low(3, 1, kr)

        def dve_final(dve):
            def finish(n):
                dve.wait_ge(gate_s, n + 1)
                nc.vector.tensor_tensor(gz[n % 2], gz[n % 2], ch5(pp, n), ALU.mult).then_inc(gate_p, 1)
                dve.wait_ge(gate_p, n + 1)
                nc.vector.tensor_tensor(h[:, n, :], h[:, n, :], gz[n % 2], ALU.add).then_inc(h_final, 1)

            dve.wait_ge(rst, 4)
            dve.wait_ge(pp_in, 32)
            for n in range(KT):
                u = Unit(U_GATE + n)
                if exists(u.plus(2)):
                    split_lo(dve, u.plus(2))
                dve.wait_ge(unit_done, u.number(1))
                nc.vector.tensor_tensor(gz[n % 2], acc[u.const % 2][:], rstd, ALU.mult).then_inc(evac[u.const % 2], 1)
                finish(n)

        @block.vector
        def _(dve):
            nc.vector.memset(xpad[:, 0:3], 0.0).then_inc(zp, 1)
            split_lo(dve, Unit(0))
            dve.wait_ge(s_par, 16)
            for k in range(KT):
                dve.wait_ge(x_hi, k + 1)
                nc.vector.scalar_tensor_tensor(out=yl[:, k, :], in0=h[:, k, :], scalar=pc("mix_g", k),
                                               in1=yh[:, k, :].bitcast(F32), op0=ALU.mult, op1=ALU.subtract).then_inc(x_lo, 1)
            dve.wait_ge(g_act, 1)
            nc.vector.tensor_tensor(wl[3][:, 0:P], W(21)[:, 0:P], wh[3][:, 0:P].bitcast(F32), ALU.subtract).then_inc(g_dve, 1)
            split_lo(dve, Unit(1))
            nc.vector.tensor_tensor(par[:, NPAR:NPAR + KT], par[:, PC["fin_g"][0]:PC["fin_g"][1]],
                                    par[:, PC["n1_g"][0]:PC["n1_g"][1]], ALU.mult)
            nc.vector.tensor_scalar(par[:, NPAR + KT:NPAR + KT + 1], pc("q_g"), HD ** -0.5, None, ALU.mult)
            dve.wait_ge(rst, 1)
            dve_gdn(dve, 0, False, True)
            dve_gdn(dve, 1, True, True)
            with dve.Fori(2, H) as i:
                dve_gdn(dve, i, True, True)
            dve_gdn(dve, H, True, False)
            dve_output(dve, H)
            for n in range(KT):
                u = Unit(U_OUT1 + n)
                for ahead in OUT_AHEAD[n]:
                    split_lo(dve, u.plus(ahead))
                dve_stream_tile(dve, n, u, "mlp_g")
            dve_mlp(dve, U_FF1, 0, True, False, None)
            with dve.Fori(1, FF_GROUPS - 1) as g:
                dve_mlp(dve, U_FF1, g, False, False, None)
            dve_mlp(dve, U_FF1, FF_GROUPS - 1, False, True, "fn_g")
            dve_att(dve, 0, False, True)
            dve_att(dve, 1, True, True)
            with dve.Fori(2, PAIRS) as i:
                dve_att(dve, i, True, True)
            dve_att(dve, PAIRS, True, True)
            dve_conv_sgu(dve)
            for n in range(KT):
                u = Unit(U_OUT2 + n)
                split_lo(dve, u.plus(2))
                dve_stream_tile(dve, n, u, "n2_g")
            dve_mlp(dve, U_FF2, 0, True, False, None)
            with dve.Fori(1, FF_GROUPS - 1) as g:
                dve_mlp(dve, U_FF2, g, False, False, None)
            dve_mlp(dve, U_FF2, FF_GROUPS - 1, False, True, "n3_g")
            dve_final(dve)



def constants():
    j, i = np.mgrid[0:P, 0:P]
    keep = np.concatenate([j == i, j >= 0, j <= i], axis=1).astype(np.float32)
    levels = []
    for n in range(LEVELS):
        s = 1 << n
        levels.append((j // (2 * s) == i // (2 * s)) & (j // s % 2 == 0) & (i // s % 2 == 1))
    levels = np.where(np.concatenate(levels, axis=1), np.float32(-1), np.float32(0))
    second = np.concatenate([np.where(j >= i, -1.0, 0.0), np.full((P, P), -1.0), np.where(i <= j, NEG, 0.0),
                             np.where(j // HD == i // HD, 1.0, 0.0)], axis=1).astype(np.float32)
    return keep, levels, second


def pack(weights):
    def unit(w, col, row=0):
        return w[row:row + D, col:col + P].reshape(KT, P, P).transpose(1, 0, 2).reshape(P, D)

    w_in, w_out, w1, w2, w_in2, w_out2, w12, w22, proj, gate = weights
    units = [unit(w_in, sec * D + i * P) for i in range(H) for sec in (1, 0, 2, 3)]
    units += [unit(w_out, m * P) for m in range(KT)]
    mlp = [[unit(a, g * D + n * P) for n in range(KT)] + [unit(b, n * P, g * D) for n in range(KT)]
           for a, b in ((w1, w2), (w12, w22)) for g in range(FF_GROUPS)]
    units += sum(mlp[:FF_GROUPS], [])
    units += [proj[:, n * T:(n + 1) * T].reshape(2, P, T).transpose(1, 0, 2).reshape(P, D) for n in range(2)]
    heads = 2 * HD * PAIRS
    conv = 2 * P
    for j in range(PAIRS):
        units += [unit(w_in2, 3 * conv + sec * heads + j * P) for sec in range(4)]
    units += [unit(w_in2, sec * conv + t * P) for t in range(2) for sec in (1, 2, 0)]
    units += [unit(w_out2, m * P) for m in range(KT)]
    units += sum(mlp[FF_GROUPS:], [])
    units += [unit(gate, m * P) for m in range(KT)]
    assert len(units) == U_END
    return np.stack(units, axis=1)


def kernel(**x):
    import concourse.bacc as bacc
    from concourse.bass_utils import run_bass_kernel_spmd

    return launch(x, bacc, run_bass_kernel_spmd)


def launch(x, bacc, run):
    def tiles(v):
        return np.asarray(v).reshape(-1, P).T

    x = {k: np.asarray(v) for k, v in x.items()}
    cw = x["gdn_conv_w"][0].reshape(TAPS, 3, H, P).transpose(3, 1, 0, 2).reshape(P, -1)
    cw2 = x["conv_w_2"][0].reshape(TAPS2, 2, P).transpose(2, 1, 0).reshape(P, -1)
    params = np.concatenate([
        tiles(x["norm_mix_g"][0]), tiles(x["norm_mlp_g"][0]), tiles(x["final_norm_g"]), tiles(x["norm1_g_2"][0]),
        tiles(x["norm2_g_2"][0]), tiles(x["norm3_g_2"][0]), cw, cw2, tiles(x["gdn_o_norm_g"][0]),
        tiles(np.tile(x["q_norm_g_2"][0], 2)), tiles(np.tile(x["k_norm_g_2"][0], 2)), tiles(x["sgu_norm_g_2"][0]),
        np.broadcast_to(x["gdn_a_log"][0], (P, H)), np.broadcast_to(x["gdn_dt_bias"][0], (P, H)),
    ], axis=1)
    keep, levels, second = constants()
    sgu_w = x["sgu_w_2"][0].transpose(2, 0, 1).reshape(P, -1)
    sgu_b = np.repeat(x["sgu_b_2"][0].reshape(2, 2, P), HD, axis=1).transpose(1, 0, 2).reshape(P, -1)
    arrays = {
        "xT": x["x"][0].T, "pT": x["p_2"][0, 0].T, "params": params, "keep": keep, "levels": levels,
        "cst2": np.concatenate([second, sgu_w, sgu_b], axis=1),
        "w_ab": x["gdn_w_in"][0][:, 4 * D:].reshape(KT, P, 2 * H).transpose(1, 0, 2).reshape(P, -1),
        "weights": pack([x[k][0] for k in ("gdn_w_in", "gdn_w_out", "mlp_w1", "mlp_w2", "w_in_2", "w_out_2",
                                           "w_ff1_2", "w_ff2_2", "w_ple_proj_2", "w_ple_gate_2")]),
    }
    arrays = {k: np.ascontiguousarray(v) for k, v in arrays.items()}
    nc = bacc.Bacc("TRN2", target_bir_lowering=False, num_devices=1)
    a = {k: nc.dram_tensor("in_" + k, v.shape, mybir.dt.from_np(v.dtype), kind="ExternalInput").ap() for k, v in arrays.items()}
    out = nc.dram_tensor("outT", (D, T), F32, kind="ExternalOutput").ap()
    build(nc, a, out)
    r = run(nc, [{"in_" + k: v for k, v in arrays.items()}], core_ids=[0])
    return np.ascontiguousarray(r.results[0]["outT"].T)[None]
```
